# Optimizing a Trainium2 kernel written in Bass

```python
import math
import jax
import jax.numpy as jnp
from jax import lax
import numpy as np

D_MODEL = 2048
BATCH = 1
SEQ = 256
DEPTH = 2

N_MIXERS = 2
N_ATTN_LAYERS = (DEPTH + 1) // 2
N_CONV_LAYERS = DEPTH // 2
HEAD_DIM = 128
N_HEADS = D_MODEL // HEAD_DIM
N_KV_HEADS = 4
N_REP = N_HEADS // N_KV_HEADS
IDX_HEADS = 16
IDX_DIM = 64
TOPK_MAX = 256
Q_BLOCK = 128
CONV_WIDTH = 3
FFN_HIDDEN = int(math.ceil(8 * D_MODEL / 3 / 256) * 256)
ROPE_THETA = 10000.0
RMS_EPS = 1e-6

Q_COLS = N_HEADS * HEAD_DIM
KV_COLS = N_KV_HEADS * HEAD_DIM
QI_COLS = IDX_HEADS * IDX_DIM
ATTN_IN_COLS = Q_COLS + 2 * KV_COLS + QI_COLS + IDX_DIM + IDX_HEADS
ATTN_SPLITS = (Q_COLS, Q_COLS + KV_COLS, Q_COLS + 2 * KV_COLS,
               Q_COLS + 2 * KV_COLS + QI_COLS, Q_COLS + 2 * KV_COLS + QI_COLS + IDX_DIM)

kernel_name = "hybrid_dsa_shortconv_swiglu"

def _rmsnorm(x, g):
    xf = x.astype(jnp.float32)
    y = xf * lax.rsqrt(jnp.mean(xf * xf, axis=-1, keepdims=True) + RMS_EPS)
    return (y * g.astype(jnp.float32)).astype(x.dtype)

def _rope_tables(seq_len, dim):
    inv_freq = 1.0 / (ROPE_THETA ** (jnp.arange(0, dim, 2, dtype=jnp.float32) / dim))
    ang = jnp.arange(seq_len, dtype=jnp.float32)[:, None] * inv_freq[None, :]
    return jnp.cos(ang)[None, :, None, :], jnp.sin(ang)[None, :, None, :]

def _rope(x, cos, sin):
    xf = x.astype(jnp.float32)
    x1, x2 = jnp.split(xf, 2, axis=-1)
    out = jnp.concatenate([x1 * cos - x2 * sin, x2 * cos + x1 * sin], axis=-1)
    return out.astype(x.dtype)

def _dsa_mixer(h, w_in, q_norm, k_norm, w_out):
    B, S, _ = h.shape
    proj = h @ w_in
    q, k, v, qi, ki, wi = jnp.split(proj, ATTN_SPLITS, axis=-1)
    q = q.reshape(B, S, N_HEADS, HEAD_DIM)
    k = k.reshape(B, S, N_KV_HEADS, HEAD_DIM)
    v = v.reshape(B, S, N_KV_HEADS, HEAD_DIM)
    qi = qi.reshape(B, S, IDX_HEADS, IDX_DIM)
    ki = ki.reshape(B, S, 1, IDX_DIM)

    cos_h, sin_h = _rope_tables(S, HEAD_DIM)
    cos_i, sin_i = _rope_tables(S, IDX_DIM)
    q = _rope(_rmsnorm(q, q_norm), cos_h, sin_h)
    k = _rope(_rmsnorm(k, k_norm), cos_h, sin_h)
    qi = _rope(qi, cos_i, sin_i)
    ki = _rope(ki, cos_i, sin_i)[:, :, 0, :]
    wi = wi * (IDX_HEADS ** -0.5 * IDX_DIM ** -0.5)

    topk = min(TOPK_MAX, S // 4)
    key_pos = jnp.arange(S)
    batch_idx = jnp.arange(B)[:, None, None]
    scale = HEAD_DIM ** -0.5

    def block(qb):
        start = qb * Q_BLOCK
        tq = start + jnp.arange(Q_BLOCK)
        qi_b = lax.dynamic_slice_in_dim(qi, start, Q_BLOCK, axis=1)
        wi_b = lax.dynamic_slice_in_dim(wi, start, Q_BLOCK, axis=1)
        q_b = lax.dynamic_slice_in_dim(q, start, Q_BLOCK, axis=1)
        rel = jax.nn.relu(jnp.einsum('bqhd,bsd->bqhs', qi_b, ki).astype(jnp.float32))
        idx_score = jnp.einsum('bqhs,bqh->bqs', rel, wi_b.astype(jnp.float32))
        causal = key_pos[None, None, :] <= tq[None, :, None]
        idx_score = jnp.where(causal, idx_score, -jnp.inf)
        _, sel = lax.top_k(idx_score, topk)
        k_sel = k[batch_idx, sel]
        v_sel = v[batch_idx, sel]
        q_g = q_b.reshape(B, Q_BLOCK, N_KV_HEADS, N_REP, HEAD_DIM)
        logits = jnp.einsum('bqgrd,bqkgd->bqgrk', q_g, k_sel).astype(jnp.float32) * scale
        valid = (sel <= tq[None, :, None])[:, :, None, None, :]
        p = jax.nn.softmax(jnp.where(valid, logits, -jnp.inf), axis=-1).astype(v.dtype)
        o = jnp.einsum('bqgrk,bqkgd->bqgrd', p, v_sel)
        return o.reshape(B, Q_BLOCK, N_HEADS * HEAD_DIM)

    o = lax.map(block, jnp.arange(S // Q_BLOCK))
    o = jnp.transpose(o, (1, 0, 2, 3)).reshape(B, S, N_HEADS * HEAD_DIM)
    return o @ w_out

def _shortconv_mixer(h, w_in, conv_w, w_out):
    proj = h @ w_in
    b_gate, c_gate, u = jnp.split(proj, 3, axis=-1)
    z = c_gate * u
    zp = jnp.pad(z, ((0, 0), (CONV_WIDTH - 1, 0), (0, 0)))
    y = conv_w[0] * zp[:, :-2] + conv_w[1] * zp[:, 1:-1] + conv_w[2] * zp[:, 2:]
    return (b_gate * y) @ w_out

def _swiglu(h, w_gate, w_up, w_down):
    return (jax.nn.silu(h @ w_gate) * (h @ w_up)) @ w_down

def setup_inputs(seed: int = 0) -> dict:
    key = jax.random.key(seed)
    ks = jax.random.split(key, 16)
    f32 = jnp.float32

    def w(k, shape, fan_in):
        return jax.random.normal(k, shape, f32) * (fan_in ** -0.5)

    def gain(k, shape):
        return 1.0 + 0.02 * jax.random.normal(k, shape, f32)

    na, nc = N_ATTN_LAYERS, N_CONV_LAYERS
    return {
        "x": jax.random.normal(ks[0], (BATCH, SEQ, D_MODEL), f32),
        "attn_norm": gain(ks[1], (na, D_MODEL)),
        "attn_w_in": w(ks[2], (na, D_MODEL, ATTN_IN_COLS), D_MODEL),
        "attn_q_norm": gain(ks[3], (na, HEAD_DIM)),
        "attn_k_norm": gain(ks[4], (na, HEAD_DIM)),
        "attn_w_out": w(ks[5], (na, N_HEADS * HEAD_DIM, D_MODEL), N_HEADS * HEAD_DIM),
        "conv_norm": gain(ks[6], (nc, D_MODEL)),
        "conv_w_in": w(ks[7], (nc, D_MODEL, 3 * D_MODEL), D_MODEL),
        "conv_w": w(ks[8], (nc, CONV_WIDTH, D_MODEL), CONV_WIDTH),
        "conv_w_out": w(ks[9], (nc, D_MODEL, D_MODEL), D_MODEL),
        "ffn_norm": gain(ks[10], (DEPTH, D_MODEL)),
        "ffn_w_gate": w(ks[11], (DEPTH, D_MODEL, FFN_HIDDEN), D_MODEL),
        "ffn_w_up": w(ks[12], (DEPTH, D_MODEL, FFN_HIDDEN), D_MODEL),
        "ffn_w_down": w(ks[13], (DEPTH, FFN_HIDDEN, D_MODEL), FFN_HIDDEN),
    }

def reference(x, attn_norm, attn_w_in, attn_q_norm, attn_k_norm, attn_w_out,
              conv_norm, conv_w_in, conv_w, conv_w_out,
              ffn_norm, ffn_w_gate, ffn_w_up, ffn_w_down):
    for i in range(DEPTH):
        j = i // N_MIXERS
        if i % N_MIXERS == 0:
            x = x + _dsa_mixer(_rmsnorm(x, attn_norm[j]), attn_w_in[j], attn_q_norm[j],
                               attn_k_norm[j], attn_w_out[j])
        else:
            x = x + _shortconv_mixer(_rmsnorm(x, conv_norm[j]), conv_w_in[j], conv_w[j], conv_w_out[j])
        x = x + _swiglu(_rmsnorm(x, ffn_norm[i]), ffn_w_gate[i], ffn_w_up[i], ffn_w_down[i])
    return x


_drawn_inputs = setup_inputs


def setup_inputs(seed=0):
    import zlib

    import numpy as np

    out = dict(_drawn_inputs(seed))
    spreads = {}
    factors = {'attn_q_norm': 8.0, 'attn_k_norm': 8.0, 'conv_norm': 2.828, 'ffn_norm': 3.277}
    for name, (base, spread) in spreads.items():
        noise = np.random.default_rng([zlib.crc32(name.encode()), seed]).standard_normal(out[name].shape)
        drawn = base * np.exp(spread * noise) if base else spread * noise
        out[name] = jnp.asarray(drawn.astype(out[name].dtype))
    for name, factor in factors.items():
        out[name] = (out[name] * factor).astype(out[name].dtype)
    return out
```

```python
from contextlib import ExitStack

import numpy as np

import concourse.bass as bass
from concourse import mybir
from concourse.alu_op_type import AluOpType as ALU

ACT = mybir.ActivationFunctionType
F32 = mybir.dt.float32
F32R = mybir.dt.float32r
AX_X = mybir.AxisListType.X

P = 128
TOK = 256
D = 2048
KT = D // P
HEADS, KV, REP, HD = 16, 4, 4, 128
IH, ID = 16, 64
F = 5632
FT = F // P
TOPK = 64
EPS = 1e-6
RING = 4
SLOT = 1024
WIDE, NARROW = 512, 256
COLS = ((0, 128), (128, 384))
FILL = -3.0e38
TAKEN = -3.3e38
DROP = -1.0e30

S_KI = 0
S_QI = S_KI + 4
S_QKV = S_QI + 4 * 4
S_AO = S_QKV + KV * 12
S_GU0 = S_AO + 4 * 8
S_DN0 = S_GU0 + (FT // 4) * 16
S_CV = S_DN0 + 4 * 22
S_CO = S_CV + 8 * 12
S_GU1 = S_CO + 4 * 8
S_DN1 = S_GU1 + (FT // 4) * 16
S_END = S_DN1 + 4 * 22


def trunk(nc, x, attn_w_in, attn_w_out, conv_w_in, conv_w_out, w_gate, w_up, w_down,
          gains, head_gains, conv_taps, tables, mats, bounds, out):
    with ExitStack() as ctx:
        def sb(name, shape, dt=F32, stack=ctx):
            return stack.enter_context(nc.sbuf_tensor(name, shape, dt))

        def sem(name):
            return ctx.enter_context(nc.semaphore(name))

        stage = sb("stage", [P, RING, SLOT])
        w_hi = sb("w_hi", [P, RING, SLOT], F32R)
        w_lo = sb("w_lo", [P, RING, SLOT], F32R)
        xs = sb("xs", [P, KT, 2 * TOK], F32R)
        res = sb("res", [P, KT, TOK])
        gain = sb("gain", [P, 4, KT])
        hgain = sb("hgain", [P, 2])
        taps = sb("taps", [P, 3, KT])
        mat = sb("mat", [P, 2, P])
        cross = sb("cross", [P, 4, TOK])
        total = sb("total", [P, 4, TOK])
        gated = sb("gated", [P, 4, TOK])
        square = sb("square", [P, 4, TOK])
        sums = sb("sums", [P, 4, TOK])
        colsum = sb("colsum", [P, TOK])
        rstd = sb("rstd", [P, TOK])
        eps = sb("eps", [P, 1])

        part = ExitStack()
        sb("head_outputs", [P, KT, 2 * TOK], F32R, stack=part)
        tab = sb("tab", [P, 4, TOK], stack=part)
        mat_a = sb("mat_a", [P, 5, P], stack=part)
        bound = sb("bound", [P, 2, 384], stack=part)
        kiwi = sb("kiwi", [P, TOK], stack=part)
        kir = sb("kir", [P, TOK], stack=part)
        qir = sb("qir", [P, 2, TOK], stack=part)
        wt = sb("wt", [P, 2, IH], stack=part)
        score = sb("score", [P, 384], stack=part)
        top8 = sb("top8", [P, 8, 2, 8], stack=part)
        mask = sb("mask", [P, 384], stack=part)
        raw = sb("raw", [P, 6, TOK], stack=part)
        k_sq = sb("k_sq", [P, TOK], stack=part)
        k_gn = sb("k_gn", [P, TOK], stack=part)
        k_rt = sb("k_rt", [P, TOK], stack=part)
        kr = sb("kr", [P, TOK], stack=part)
        qr = sb("qr", [P, 4, TOK], stack=part)
        vt = sb("vt", [P, 2, HD], stack=part)
        peak = sb("peak", [P, 2, 4], stack=part)
        npeak = sb("npeak", [P, 2, 4], stack=part)
        den = sb("den", [P, 2, 4], stack=part)
        rden = sb("rden", [P, 2, 4], stack=part)
        early = ExitStack()
        xin = sb("xin", [P, 2, D], stack=early)
        early.close()
        late = ExitStack()
        prob = sb("prob", [P, 4, 384], stack=late)
        pt = sb("pt", [P, 4, 384], stack=late)
        late.close()
        part.close()
        whole = ExitStack()
        hs = sb("hs", [P, FT, 2 * TOK], F32R, stack=whole)
        whole.close()
        rows = sb("rows", [P, 2, D])

        rms = colsum
        ytap = square[:, 0:2, :]
        z = sums[:, :, :].rearrange("p m t -> p (m t)")[:, 0:2 * (TOK + 2)].rearrange("p (m t) -> p m t", m=2)

        def f32(ap):
            return ap.bitcast(F32)

        ps = ctx.enter_context(nc.psum_tensor("ps", [P, 8, 512], F32))

        IDENT, MEAN_D = (mat[:, i, :] for i in range(2))
        MEAN_H, ROT_H, ROT_I, DUP, DUP_ROT = (mat_a[:, i, :] for i in range(5))

        in_x = sem("in_x")
        in_small = sem("in_small")
        loaded = [sem(f"loaded{i}") for i in range(RING)]
        v_loaded = [sem(f"v_loaded{i}") for i in range(RING)]
        hi_done = sem("hi_done")
        lo_done = sem("lo_done")
        slot_used = sem("slot_used")
        const_set = sem("const_set")
        x_turned = sem("x_turned")
        res_cross = sem("res_cross")
        res_summed = sem("res_summed")
        res_added = sem("res_added")
        res_squared = sem("res_squared")
        res_gained = sem("res_gained")
        res_hi = sem("res_hi")
        xs_ready = sem("xs_ready")
        sums_done = sem("sums_done")
        stat_sum = sem("stat_sum")
        stat_made = sem("stat_made")
        stat_root = sem("stat_root")
        rstd_ready = sem("rstd_ready")
        ki_scaled = sem("ki_scaled")
        ki_turned = sem("ki_turned")
        ki_cos = sem("ki_cos")
        ki_ready = sem("ki_ready")
        wt_ready = sem("wt_ready")
        qi_cross = sem("qi_cross")
        qi_summed = sem("qi_summed")
        qi_scaled = sem("qi_scaled")
        qi_turned = sem("qi_turned")
        qi_cos = sem("qi_cos")
        qi_sin = sem("qi_sin")
        qi_ready = sem("qi_ready")
        score_made = sem("score_made")
        low_read = sem("low_read")
        high_read = sem("high_read")
        score_step = sem("score_step")
        top_step = sem("top_step")
        mask_ready = sem("mask_ready")
        qkv_cross = sem("qkv_cross")
        qkv_summed = sem("qkv_summed")
        qkv_scaled = sem("qkv_scaled")
        k_squared = sem("k_squared")
        k_gained = sem("k_gained")
        k_made = sem("k_made")
        k_root = sem("k_root")
        k_inv = sem("k_inv")
        k_cos = sem("k_cos")
        k_sin = sem("k_sin")
        k_roped = sem("k_roped")
        k_ready = sem("k_ready")
        v_made = sem("v_made")
        v_ready = sem("v_ready")
        q_squared = sem("q_squared")
        q_gained = sem("q_gained")
        q_made = sem("q_made")
        q_root = sem("q_root")
        q_inv = sem("q_inv")
        q_cos = sem("q_cos")
        q_sin = sem("q_sin")
        q_roped = sem("q_roped")
        q_ready = sem("q_ready")
        s_made = sem("s_made")
        logit_ready = sem("logit_ready")
        peak_done = sem("peak_done")
        npeak_done = sem("npeak_done")
        exp_done = sem("exp_done")
        rden_done = sem("rden_done")
        prob_ready = sem("prob_ready")
        pt_made = sem("pt_made")
        o_made = sem("o_made")
        o_hi = sem("o_hi")
        gate_cross = sem("gate_cross")
        gate_summed = sem("gate_summed")
        gate_scaled = sem("gate_scaled")
        gate_silu = sem("gate_silu")
        up_cross = sem("up_cross")
        up_summed = sem("up_summed")
        up_scaled = sem("up_scaled")
        hidden_done = sem("hidden_done")
        hidden_hi = sem("hidden_hi")
        hidden_ready = sem("hidden_ready")
        cv_cross = sem("cv_cross")
        cv_summed = sem("cv_summed")
        cv_scaled = sem("cv_scaled")
        z_ready = sem("z_ready")
        tap_step = sem("tap_step")
        y_done = sem("y_done")
        y_hi = sem("y_hi")
        y_ready = sem("y_ready")
        row_made = sem("row_made")
        row_ready = sem("row_ready")
        row_ready_act = sem("row_ready_act")
        stored = sem("stored")

        def bcast(ap, tiles):
            return ap.unsqueeze(1).to_broadcast([P, tiles, ap.shape[1]])

        def per_tile(ap, width):
            return ap.unsqueeze(2).to_broadcast([P, ap.shape[1], width])

        block = ctx.enter_context(nc.Block())

        @block.sync
        def _(sp):
            def load(n, pos, rows_of, width):
                k = rows_of.shape[0] // P
                if not isinstance(n, int) or n >= RING:
                    sp.wait_ge(lo_done, n - (RING - 1))
                dst = stage[:, pos, 0:k * width].rearrange("p (k n) -> p k n", k=k)
                sp.dma_start(dst, rows_of.rearrange("(k p) n -> p k n", p=P)).then_inc(loaded[pos], 16)

            def load_block(n, w, base, col, width, tiles):
                per = SLOT // width if width >= NARROW else 4
                for s in range(tiles // per):
                    load(n + s, s % RING, w[s * per * P:(s + 1) * per * P, base:][:, bass.ds(col, width)], width)

            sp.dma_start(xin[:, 0, :], x[0:P, :]).then_inc(in_x, 16)
            sp.dma_start(xin[:, 1, :], x[P:TOK, :]).then_inc(in_x, 16)
            for dst, src in ((mat, mats[:, 0:2, :]), (mat_a, mats[:, 2:7, :]), (gain, gains), (tab, tables), (bound, bounds),
                             (hgain, head_gains), (taps, conv_taps)):
                sp.dma_start(dst.ap(), src).then_inc(in_small, 16)

            w_in = attn_w_in
            load_block(S_KI, w_in, D + 2 * KV * HD + IH * ID, 0, ID + IH, KT)
            with sp.Fori(0, 4) as i:
                load_block(S_QI + 4 * i, w_in, D + 2 * KV * HD, NARROW * i, NARROW, KT)
            with sp.Fori(0, KV) as g:
                n = S_QKV + 12 * g
                for s in range(4):
                    rows4 = slice(s * 4 * P, (s + 1) * 4 * P)
                    sp.wait_ge(lo_done, n + s - (RING - 1))
                    dst = stage[:, s, :].rearrange("p (k n) -> p k n", k=4)
                    for side, arrived in ((0, loaded[s]), (1, v_loaded[s])):
                        src = w_in[rows4, D + side * KV * HD:][:, bass.ds(HD * g, HD)]
                        sp.dma_start(dst[:, :, side * HD:(side + 1) * HD],
                                     src.rearrange("(k p) n -> p k n", p=P)).then_inc(arrived, 16)
                load_block(n + 4, w_in, 0, WIDE * g, NARROW, KT)
                load_block(n + 8, w_in, NARROW, WIDE * g, NARROW, KT)

            def load_wide(first, w, tiles):
                slots = tiles // 2
                with sp.Fori(0, 2) as i:
                    for u in range(2):
                        for s in range(slots):
                            load(first + 2 * slots * i + u * slots + s, (u * slots + s) % RING,
                                 w[s * 2 * P:(s + 1) * 2 * P, WIDE * u:][:, bass.ds(2 * WIDE * i, WIDE)], WIDE)

            def load_ffn(first, layer):
                with sp.Fori(0, FT // 4) as i:
                    load_block(first + 16 * i, w_gate[layer], 0, WIDE * i, WIDE, KT)
                    load_block(first + 16 * i + 8, w_up[layer], 0, WIDE * i, WIDE, KT)

            load_wide(S_AO, attn_w_out, KT)
            load_ffn(S_GU0, 0)
            load_wide(S_DN0, w_down[0], FT)
            with sp.Fori(0, 8) as i:
                for u, base in enumerate((D, 2 * D, 0)):
                    col = NARROW * i if u < 2 else (P * i) * 2
                    load_block(S_CV + 12 * i + 4 * u, conv_w_in, base, col, NARROW, KT)
            load_wide(S_CO, conv_w_out, KT)
            load_ffn(S_GU1, 1)
            load_wide(S_DN1, w_down[1], FT)

            for a in range(2):
                sp.wait_ge(row_ready if a == 0 else row_ready_act, 4)
                sp.dma_start(out[a * P:(a + 1) * P, :], rows[:, a, :]).then_inc(stored, 16)
            sp.wait_ge(stored, 32)

        @block.tensor
        def _(pe):
            def stream(n, banks, width, tiles, moving, ready=None, count=P, place=0):
                per = SLOT // width if width >= NARROW else 4
                step = width if width >= NARROW else count
                for s in range(tiles // per):
                    pe.wait_ge(lo_done, n + s + 1)
                    for kk in range(per):
                        k = s * per + kk
                        if ready is not None:
                            ready(k)
                        rhs = moving(k)
                        for m in range((width + P - 1) // P):
                            at = slice(kk * step + m * P, kk * step + m * P + count)
                            bank = ps[0:count, banks[m], :]
                            slot = (place + s) % RING
                            full = (bank, w_hi[:, slot, at], rhs)
                            low = (bank[:, TOK:], w_lo[:, slot, at], rhs[:, 0:TOK])
                            last = k == tiles - 1
                            if last:
                                pe.matmul(*low, start=False, stop=False)
                                mm = pe.matmul(*full, start=False, stop=True)
                            else:
                                pe.matmul(*full, start=k == 0, stop=False)
                                mm = pe.matmul(*low, start=False, stop=False)
                    mm.then_inc(slot_used, 1)

            low_banks, high_banks = (0, 1, 2, 3), (4, 5, 6, 7)

            def xs_tile(k):
                return xs[:, k, :]

            def hs_tile(k):
                return hs[:, k, :]

            def xs_wait(stage_no):
                def ready(k):
                    if k % 4 == 0:
                        pe.wait_ge(xs_ready, 4 * stage_no + k // 4 + 1)
                return ready

            def stat(no):
                pe.wait_ge(stat_sum, no + 1)
                pe.matmul(ps[:, 7, 0:TOK], MEAN_D, colsum[:, :], start=True, stop=True).then_inc(stat_made, 1)
                pe.wait_ge(stat_root, no + 1)

            pe.wait_ge(in_x, 32)
            pe.wait_ge(in_small, 112)
            for j in range(4):
                if j >= 2:
                    pe.wait_ge(res_added, j - 1)
                for m in range(4):
                    for a in range(2):
                        mm = pe.transpose(ps[:, 4 * (j % 2) + m, a * P:(a + 1) * P],
                                          xin[:, a, (4 * j + m) * P:(4 * j + m + 1) * P], IDENT)
                mm.then_inc(x_turned, 1)
            pe.wait_ge(res_added, 4)

            stream(S_KI, (0,), ID + IH, KT, xs_tile, xs_wait(0), count=ID + IH)
            stat(0)
            pe.wait_ge(ki_scaled, 1)
            pe.matmul(ps[:, 6, 0:TOK], DUP[0:ID, :], kiwi[0:ID, :], start=True, stop=True)
            pe.matmul(ps[:, 6, TOK:], DUP_ROT[0:ID, :], kiwi[0:ID, :], start=True, stop=True)
            for a in range(2):
                mm = pe.transpose(ps[:, 7, a * P:a * P + 80], kiwi[0:80, a * P:(a + 1) * P], IDENT[0:80, 0:80])
            mm.then_inc(ki_turned, 1)

            with pe.Fori(0, 4) as i:
                pe.wait_ge(qi_summed, i + 1)
                stream(S_QI + 4 * i, (0, 1), NARROW, KT, xs_tile)
                pe.wait_ge(qi_scaled, i + 1)
                pe.wait_ge(high_read, 1)
                for m in range(2):
                    mm = pe.matmul(ps[:, 6, m * TOK:(m + 1) * TOK], ROT_I, total[:, m, :], start=True, stop=True)
                mm.then_inc(qi_turned, 1)
                pe.wait_ge(qi_ready, i + 1)
                pe.wait_ge(ki_ready, 1)
                pe.wait_ge(low_read, i + 1)
                for h in range(4):
                    half = slice(ID * (h % 2), ID * (h % 2) + ID)
                    for a, (c0, c1) in enumerate(COLS):
                        mm = pe.matmul(ps[:, 2 + h, c0:c1], qir[half, h // 2, a * P:(a + 1) * P],
                                       kir[half, 0:c1 - c0], start=True, stop=True)
                mm.then_inc(score_made, 1)

            with pe.Fori(0, KV) as g:
                n = S_QKV + 12 * g
                pe.wait_ge(low_read, g + 5)
                pe.wait_ge(qi_summed, 5)
                stream(n, (0, 1), NARROW, KT, xs_tile)
                stream(n + 4, (2, 3), NARROW, KT, xs_tile)
                pe.wait_ge(high_read, g + 1)
                pe.wait_ge(qi_sin, 4)
                pe.wait_ge(wt_ready, 1)
                stream(n + 8, (4, 5), NARROW, KT, xs_tile)
                pe.wait_ge(k_squared, g + 1)
                pe.matmul(ps[:, 6, 0:TOK], MEAN_H, k_sq[:, :], start=True, stop=True)
                pe.wait_ge(k_gained, g + 1)
                pe.matmul(ps[:, 6, TOK:], ROT_H, k_gn[:, :], start=True, stop=True).then_inc(k_made, 1)
                for a in range(2):
                    mm = pe.transpose(ps[:, 7, a * P:(a + 1) * P], raw[:, 1, a * P:(a + 1) * P], IDENT)
                mm.then_inc(v_made, 1)
                pe.wait_ge(q_squared, g + 1)
                for m in range(4):
                    pe.matmul(ps[:, m, 0:TOK], MEAN_H, square[:, m, :], start=True, stop=True)
                pe.wait_ge(q_gained, g + 1)
                for m in range(4):
                    mm = pe.matmul(ps[:, m, TOK:], ROT_H, gated[:, m, :], start=True, stop=True)
                mm.then_inc(q_made, 1)
                pe.wait_ge(k_ready, g + 1)
                pe.wait_ge(q_ready, g + 1)
                for h in range(REP):
                    for a, (c0, c1) in enumerate(COLS):
                        mm = pe.matmul(ps[:, h, c0:c1], qr[:, h, a * P:(a + 1) * P], kr[:, 0:c1 - c0],
                                       start=True, stop=True)
                mm.then_inc(s_made, 1)
                pe.wait_ge(prob_ready, 2 * g + 2)
                for h in range(REP):
                    for c in range(3):
                        mm = pe.transpose(ps[:, h, c * P:(c + 1) * P], prob[:, h, c * P:(c + 1) * P], IDENT)
                mm.then_inc(pt_made, 1)
                pe.wait_ge(low_read, g + 6)
                pe.wait_ge(v_ready, g + 1)
                for h in range(REP):
                    pe.matmul(ps[:, 4 + h, 0:TOK], vt[:, 0, :], pt[:, h, 0:TOK], start=True, stop=False)
                    mm = pe.matmul(ps[:, 4 + h, P:TOK], vt[:, 1, :], pt[:, h, TOK:384], start=False, stop=True)
                mm.then_inc(o_made, 1)

            def project(first, q, tiles, waits, ready=None):
                slots = tiles // 2
                with pe.Fori(0, 2) as i:
                    for u in range(2):
                        waits(u)
                        pe.wait_ge(res_added, 4 * q + 2 * i + u - 1)
                        stream(first + 2 * slots * i + slots * u, (low_banks, high_banks)[u], WIDE, tiles,
                               hs_tile, ready, place=slots * u % RING)

            def ao_waits(u):
                pe.wait_ge(high_read, 5)
                pe.wait_ge(low_read, 9)

            def ffn(layer, first, q):
                def body(i, first_time):
                    fb = (FT // 4) * layer + i
                    if first_time:
                        pe.wait_ge(res_summed, 4 * (q - 1) + 3)
                    else:
                        pe.wait_ge(gate_summed, fb)
                    stream(first + 16 * i, low_banks, WIDE, KT, xs_tile, xs_wait(q) if first_time else None)
                    if first_time:
                        stat(q)
                    else:
                        pe.wait_ge(up_summed, fb)
                    stream(first + 16 * i + 8, high_banks, WIDE, KT, xs_tile)
                body(0, True)
                with pe.Fori(1, FT // 4) as i:
                    body(i, False)

            def down(layer, first, q):
                blocks = (FT // 4) * (layer + 1)

                def waits(u):
                    pe.wait_ge(up_summed if u else gate_summed, blocks)

                def ready(k):
                    if k in (0, FT - 4):
                        pe.wait_ge(hidden_ready, blocks if k else blocks - 1)
                project(first, q, FT, waits, ready)

            project(S_AO, 1, KT, ao_waits)
            ffn(0, S_GU0, 1)
            down(0, S_DN0, 2)

            def conv(i, first_time):
                n = S_CV + 12 * i
                if first_time:
                    pe.wait_ge(res_summed, 7)
                else:
                    pe.wait_ge(cv_summed, 3 * i - 2)
                stream(n, (0, 1), NARROW, KT, xs_tile, xs_wait(2) if first_time else None)
                if not first_time:
                    pe.wait_ge(cv_summed, 3 * i - 1)
                stream(n + 4, (2, 3), NARROW, KT, xs_tile)
                if first_time:
                    stat(2)
                else:
                    pe.wait_ge(cv_summed, 3 * i)
                stream(n + 8, (4, 5), NARROW, KT, xs_tile)
            conv(0, True)
            with pe.Fori(1, 8) as i:
                conv(i, False)

            def co_waits(u):
                pe.wait_ge(cv_summed, 23 + u)

            def y_wait(k):
                if k in (0, KT - 2):
                    pe.wait_ge(y_ready, 8 if k else 7)

            project(S_CO, 3, KT, co_waits, y_wait)
            ffn(1, S_GU1, 3)
            down(1, S_DN1, 4)

            pe.wait_ge(res_added, 20)
            for a in range(2):
                for j in range(4):
                    for m in range(4):
                        mm = pe.transpose(ps[:, 4 * a + j, m * P:(m + 1) * P],
                                          res[:, 4 * j + m, a * P:(a + 1) * P], IDENT)
                    mm.then_inc(row_made, 1)

        @block.scalar
        def _(act):
            def split(first, slots, per_loop=0, i=0, at=0):
                for j in range(at, at + slots):
                    n = first + per_loop * i + j
                    act.wait_ge(loaded[j % RING], 16 * ((first + j) // RING + 1) + 16 * (per_loop // RING) * i)
                    if first + j >= RING:
                        act.wait_ge(slot_used, n - (RING - 1))
                    nc.scalar.activation(w_hi[:, j % RING, :], stage[:, j % RING, :], ACT.Copy).then_inc(hi_done, 1)

            def take_cross(banks, dst, n_done, sem_out, count=P):
                act.wait_ge(slot_used, n_done)
                b0, b1 = banks
                nc.scalar.activation(dst, ps[0:count, b0:b1, TOK:], ACT.Copy).then_inc(sem_out, 1)

            def stat(no):
                act.wait_ge(stat_made, no + 1)
                act.wait_ge(const_set, 1)
                nc.scalar.activation(rms[:, :], ps[:, 7, 0:TOK], ACT.Sqrt, bias=eps[:, 0:1]).then_inc(stat_root, 1)

            def res_square(rb):
                act.wait_ge(res_added, rb + 1)
                if not isinstance(rb, int) or rb:
                    act.wait_ge(sums_done, rb)
                j4 = 4 * (rb % 4)
                nc.scalar.activation(square[:, :, :], res[:, j4:j4 + 4, :], ACT.Square).then_inc(res_squared, 1)

            def res_high(rb):
                act.wait_ge(res_gained, rb + 1)
                j4 = 4 * (rb % 4)
                nc.scalar.activation(xs[:, j4:j4 + 4, 0:TOK], gated[:, :, :], ACT.Copy).then_inc(res_hi, 1)

            for j in range(4):
                res_square(j)
                res_high(j)

            for s in range(4):
                act.wait_ge(loaded[s], 16)
                nc.scalar.activation(w_hi[:, s, 0:320], stage[:, s, 0:320], ACT.Copy).then_inc(hi_done, 1)
            stat(0)
            take_cross((0, 1), cross[0:80, 0:1, :], S_QI, low_read, 80)
            act.wait_ge(ki_turned, 1)
            nc.scalar.activation(wt[:, :, :], ps[:, 7, 0:TOK].rearrange("p (a c) -> p a c", a=2)[:, :, ID:ID + IH],
                                 ACT.Copy, scale=IH ** -0.5 * ID ** -0.5).then_inc(wt_ready, 1)

            with act.Fori(0, 4) as i:
                split(S_QI, 4, 4, i)
                act.wait_ge(qi_summed, i + 1)
                take_cross((0, 2), cross[:, 0:2, :], S_QI + 4 * i + 4, qi_cross)
                act.wait_ge(score_made, i + 1)
                act.wait_ge(score_step, 8 * i + 1)
                nc.scalar.activation(prob[:, :, :], ps[:, 2:6, 0:384], ACT.Relu).then_inc(low_read, 1)

            with act.Fori(0, KV) as g:
                n = S_QKV + 12 * g
                for u in range(3):
                    if u == 0:
                        for s in range(RING):
                            act.wait_ge(v_loaded[s], 16 * g + 16)
                    split(S_QKV, 4, 12, g, 4 * u)
                    if u:
                        act.wait_ge(qkv_summed, 3 * g + u)
                    take_cross((2 * u, 2 * u + 2), cross[:, 0:2, :], n + 4 * u + 4, qkv_cross)
                act.wait_ge(qkv_scaled, 3 * g + 1)
                nc.scalar.activation(k_sq[:, :], raw[:, 0, :], ACT.Square).then_inc(k_squared, 1)
                nc.scalar.activation(k_gn[:, :], raw[:, 0, :], ACT.Copy, scale=hgain[:, 1:2]).then_inc(k_gained, 1)
                act.wait_ge(v_made, g + 1)
                nc.scalar.activation(vt[:, :, :], ps[:, 7, 0:TOK].rearrange("p (a c) -> p a c", a=2),
                                     ACT.Copy).then_inc(v_ready, 1)
                act.wait_ge(qkv_scaled, 3 * g + 3)
                nc.scalar.activation(square[:, :, :], raw[:, 2:6, :], ACT.Square).then_inc(q_squared, 1)
                nc.scalar.activation(gated[:, :, :], raw[:, 2:6, :], ACT.Copy, scale=hgain[:, 0:1]).then_inc(q_gained, 1)
                act.wait_ge(k_made, g + 1)
                nc.scalar.activation(k_rt[:, :], ps[:, 6, 0:TOK], ACT.Sqrt, bias=eps[:, 0:1]).then_inc(k_root, 1)
                act.wait_ge(q_made, g + 1)
                nc.scalar.activation(total[:, :, :], ps[:, 0:4, 0:TOK], ACT.Sqrt, bias=eps[:, 0:1]).then_inc(q_root, 1)
                act.wait_ge(npeak_done, g + 1)
                for h in range(REP):
                    for a, (c0, c1) in enumerate(COLS):
                        nc.scalar.activation(prob[:, h, c0:c1], prob[:, h, c0:c1], ACT.Exp,
                                             bias=npeak[:, a, h:h + 1],
                                             accum_out=den[:, a, h:h + 1]).then_inc(exp_done, 1)
                act.wait_ge(pt_made, g + 1)
                nc.scalar.activation(pt[:, :, :], ps[:, 0:4, 0:384], ACT.Copy).then_inc(low_read, 1)
                act.wait_ge(o_made, g + 1)
                nc.scalar.activation(hs[:, bass.ds(4 * g, 4), 0:TOK], ps[:, 4:8, 0:TOK], ACT.Copy).then_inc(o_hi, 1)

            low_banks, high_banks = (0, 4), (4, 8)

            def steps_between(first, slots, steps, per_loop=0, i=0, at=0):
                for j in range(slots):
                    split(first, 1, per_loop, i, at + j)
                    for step in steps.get(j, ()):
                        step()

            def res_steps(rb, n_done, last=False):
                def halves():
                    act.wait_ge(res_added, rb)
                    take_cross((low_banks, high_banks)[rb % 2], cross[:, :, :], n_done, res_cross)
                if last:
                    return {3: [halves]}
                return {3: [halves], 4: [lambda: res_square(rb)], 5: [lambda: res_high(rb)]}

            def project(first, q, tiles, before):
                slots = tiles // 2
                for j in range(4):
                    steps_between(first, slots, before, at=slots * j)
                    before = res_steps(4 * q + j, first + slots * (j + 1), last=q == 4)
                return before

            def hidden_tiles(fb):
                return hs[:, bass.ds(4 * fb, 4), 0:TOK]

            def gate_steps(fb, done, n_done):
                def halves():
                    if done or not isinstance(fb, int) or fb:
                        act.wait_ge(up_summed, fb + done)
                    take_cross(low_banks, cross[:, :, :], n_done, gate_cross)

                def silu():
                    act.wait_ge(gate_scaled, fb + done + 1)
                    nc.scalar.activation(gated[:, :, :], gated[:, :, :], ACT.Silu).then_inc(gate_silu, 1)
                return {11: [halves], 12: [silu]}

            def up_steps(fb, done, n_done):
                def halves():
                    act.wait_ge(gate_summed, fb + done + 1)
                    take_cross(high_banks, cross[:, :, :], n_done, up_cross)

                def high():
                    act.wait_ge(hidden_done, fb + done + 1)
                    nc.scalar.activation(hidden_tiles(fb), total[:, :, :], ACT.Copy).then_inc(hidden_hi, 1)
                return {3: [halves], 4: [high]}

            def ffn(layer, first, q, before):
                done = FT // 4 * layer
                steps_between(first, 16, before | {10: [lambda: stat(q)]} | gate_steps(0, done, first + 8))
                with act.Fori(1, FT // 4) as i:
                    steps = up_steps(i - 1, done, first + 16 * i) | gate_steps(i, done, first + 16 * i + 8)
                    steps_between(first, 16, steps, 16, i)
                return up_steps(FT // 4 - 1, done, first + 16 * (FT // 4))

            def conv_steps(i, u, n_done):
                def halves():
                    if isinstance(i, int) and i == 0 and u == 0:
                        act.wait_ge(res_added, 12)
                    else:
                        act.wait_ge(cv_summed, 3 * i + u)
                    take_cross((2 * u, 2 * u + 2), cross[:, 0:2, :], n_done, cv_cross)

                def high():
                    act.wait_ge(y_done, i + 1)
                    nc.scalar.activation(hs[:, bass.ds(2 * i, 2), 0:TOK], total[:, 0:2, :], ACT.Copy).then_inc(y_hi, 1)
                return {(7, 11, 3)[u]: [halves]} | ({4: [high]} if u == 2 else {})

            def conv(before):
                steps_between(S_CV, 12, before | conv_steps(0, 0, S_CV + 4) | {10: [lambda: stat(2)]}
                              | conv_steps(0, 1, S_CV + 8))
                with act.Fori(1, 8) as i:
                    n = S_CV + 12 * i
                    steps_between(S_CV, 12, conv_steps(i - 1, 2, n) | conv_steps(i, 0, n + 4)
                                  | conv_steps(i, 1, n + 8), 12, i)
                return conv_steps(7, 2, S_CO)

            before = project(S_AO, 1, KT, {})
            before = ffn(0, S_GU0, 1, before)
            before = project(S_DN0, 2, FT, before)
            before = conv(before)
            before = project(S_CO, 3, KT, before)
            before = ffn(1, S_GU1, 3, before)
            before = project(S_DN1, 4, FT, before)
            for step in before[3]:
                step()
            for j in range(4):
                act.wait_ge(row_made, 5 + j)
                nc.scalar.activation(rows[:, 1, WIDE * j:WIDE * (j + 1)], ps[:, 4 + j, :], ACT.Copy).then_inc(row_ready_act, 1)

        @block.vector
        def _(dve):
            tt = nc.vector.tensor_tensor

            def split(first, slots, per_loop=0, i=0, at=0):
                for j in range(at, at + slots):
                    n = first + per_loop * i + j
                    dve.wait_ge(hi_done, n + 1)
                    p = j % RING
                    tt(w_lo[:, p, :], stage[:, p, :], f32(w_hi[:, p, :]), ALU.subtract).then_inc(lo_done, 1)

            def steps_between(first, slots, steps, per_loop=0, i=0, at=0):
                for j in range(slots):
                    split(first, 1, per_loop, i, at + j)
                    for step in steps.get(j, ()):
                        step()

            def stat_sum_step(no):
                dve.wait_ge(sums_done, 4 * no + 4)
                nc.vector.tensor_reduce(colsum[:, :], sums[:, :, :].rearrange("p m t -> p t m"), AX_X,
                                        ALU.add).then_inc(stat_sum, 1)

            def rstd_step(no):
                dve.wait_ge(stat_root, no + 1)
                nc.vector.reciprocal(rstd[:, :], rms[:, :]).then_inc(rstd_ready, 1)

            def res_gain(rb):
                dve.wait_ge(res_added, rb + 1)
                q, j = divmod(rb, 4)
                tt(gated[:, :, :], res[:, 4 * j:4 * j + 4, :], per_tile(gain[:, q, 4 * j:4 * j + 4], TOK),
                   ALU.mult).then_inc(res_gained, 1)

            def res_low(rb):
                dve.wait_ge(res_hi, rb + 1)
                j4 = 4 * (rb % 4)
                tt(xs[:, j4:j4 + 4, TOK:], gated[:, :, :], f32(xs[:, j4:j4 + 4, 0:TOK]),
                   ALU.subtract).then_inc(xs_ready, 1)

            def res_sums(rb):
                dve.wait_ge(res_squared, rb + 1)
                if rb % 4:
                    dve.wait_ge(sums_done, rb)
                    tt(sums[:, :, :], sums[:, :, :], square[:, :, :], ALU.add).then_inc(sums_done, 1)
                else:
                    nc.vector.tensor_copy(sums[:, :, :], square[:, :, :]).then_inc(sums_done, 1)

            def res_steps(rb):
                q, j = divmod(rb, 4)
                bank = 4 * (rb % 2)

                def add():
                    dve.wait_ge(res_cross, rb - 3)
                    tt(total[:, :, :], ps[:, bank:bank + 4, 0:TOK], cross[:, :, :], ALU.add).then_inc(res_summed, 1)
                    dve.wait_ge(res_summed, rb - 3)
                    now = res[:, 4 * j:4 * j + 4, :]
                    tt(now, now, total[:, :, :], ALU.add).then_inc(res_added, 1)
                if q == 4:
                    return {3: [add]}
                steps = {3: [add], 4: [lambda: res_gain(rb)], 5: [lambda: res_low(rb)],
                         6: [lambda: res_sums(rb)]}
                if j == 3:
                    steps[6].append(lambda: stat_sum_step(q))
                return steps

            def project(first, q, tiles, before):
                slots = tiles // 2
                for j in range(4):
                    steps_between(first, slots, before, at=slots * j)
                    before = res_steps(4 * q + j)
                return before

            dve.wait_ge(in_small, 112)
            for j in range(4):
                dve.wait_ge(x_turned, j + 1)
                b = 4 * (j % 2)
                nc.vector.tensor_copy(res[:, 4 * j:4 * j + 4, :], ps[:, b:b + 4, 0:TOK]).then_inc(res_added, 1)
                res_gain(j)
                res_low(j)
                res_sums(j)
            stat_sum_step(0)

            COS_H, SIN_H, COS_I, SIN_I = (tab[:, i, :] for i in range(4))
            for s in range(4):
                dve.wait_ge(hi_done, s + 1)
                tt(w_lo[:, s, 0:320], stage[:, s, 0:320], f32(w_hi[:, s, 0:320]), ALU.subtract).then_inc(lo_done, 1)
            rstd_step(0)
            dve.wait_ge(low_read, 1)
            tt(kiwi[0:80, :], ps[0:80, 0, 0:TOK], cross[0:80, 0, :], ALU.add).then_inc(qi_summed, 1)
            dve.wait_ge(qi_summed, 1)
            dve.wait_ge(rstd_ready, 1)
            tt(kiwi[0:80, :], kiwi[0:80, :], rstd[0:80, :], ALU.mult).then_inc(ki_scaled, 1)
            dve.wait_ge(ki_turned, 1)
            tt(kir[:, :], ps[:, 6, 0:TOK], COS_I, ALU.mult).then_inc(ki_cos, 1)
            tt(k_sq[:, :], ps[:, 6, TOK:], SIN_I, ALU.mult).then_inc(high_read, 1)
            dve.wait_ge(ki_cos, 1)
            dve.wait_ge(high_read, 1)
            tt(kir[:, :], kir[:, :], k_sq[:, :], ALU.add).then_inc(ki_ready, 1)
            dve.wait_ge(wt_ready, 1)
            nc.vector.memset(score[:, :], 0.0).then_inc(score_step, 1)

            with dve.Fori(0, 4) as i:
                split(S_QI, 4, 4, i)
                dve.wait_ge(qi_cross, i + 1)
                two = total[:, 0:2, :]
                tt(two, ps[:, 0:2, 0:TOK], cross[:, 0:2, :], ALU.add).then_inc(qi_summed, 1)
                dve.wait_ge(qi_summed, i + 2)
                tt(two, two, bcast(rstd[:, :], 2), ALU.mult).then_inc(qi_scaled, 1)
                dve.wait_ge(qi_scaled, i + 1)
                tt(gated[:, 0:2, :], two, bcast(COS_I, 2), ALU.mult).then_inc(qi_cos, 1)
                dve.wait_ge(qi_turned, i + 1)
                tt(square[:, 0:2, :], ps[:, 6, :].rearrange("p (m t) -> p m t", m=2), bcast(SIN_I, 2),
                   ALU.mult).then_inc(qi_sin, 1)
                dve.wait_ge(qi_cos, i + 1)
                dve.wait_ge(qi_sin, i + 1)
                tt(qir[:, :, :], gated[:, 0:2, :], square[:, 0:2, :], ALU.add).then_inc(qi_ready, 1)
                dve.wait_ge(low_read, i + 2)
                for h in range(4):
                    for a, (c0, c1) in enumerate(COLS):
                        dve.wait_ge(score_step, 8 * i + max(1, 2 * h + a))
                        nc.vector.scalar_tensor_tensor(score[:, c0:c1], prob[:, h, c0:c1],
                                                       wt[:, a, bass.ds(4 * i + h, 1)], score[:, c0:c1],
                                                       ALU.mult, ALU.add).then_inc(score_step, 1)

            def top(count):
                dve.wait_ge(top_step, count)
            dve.wait_ge(score_step, 33)
            tt(score[:, :], score[:, :], bound[:, 0, :], ALU.min).then_inc(top_step, 1)
            for r in range(TOPK // 8):
                for a, (c0, c1) in enumerate(COLS):
                    top(max(1, 4 * r + a))
                    nc.vector.max(top8[:, r, a, :], score[:, c0:c1]).then_inc(top_step, 1)
                for a, (c0, c1) in enumerate(COLS):
                    top(4 * r + 2 + a)
                    nc.vector.match_replace(score[:, c0:c1], top8[:, r, a, :], score[:, c0:c1],
                                            TAKEN).then_inc(top_step, 1)
            top(TOPK // 2 + 1)
            nc.vector.tensor_scalar(mask[:, :], score[:, :], TAKEN, -DROP, ALU.is_equal, ALU.mult).then_inc(top_step, 1)
            top(TOPK // 2 + 2)
            nc.vector.tensor_scalar(mask[:, :], mask[:, :], DROP, None, ALU.add).then_inc(top_step, 1)
            top(TOPK // 2 + 3)
            tt(mask[:, :], mask[:, :], bound[:, 1, :], ALU.min).then_inc(mask_ready, 1)

            with dve.Fori(0, KV) as g:
                for u in range(3):
                    split(S_QKV, 4, 12, g, 4 * u)
                    dve.wait_ge(qkv_cross, 3 * g + u + 1)
                    two = raw[:, 2 * u:2 * u + 2, :]
                    tt(two, ps[:, 2 * u:2 * u + 2, 0:TOK], cross[:, 0:2, :], ALU.add).then_inc(qkv_summed, 1)
                    dve.wait_ge(qkv_summed, 3 * g + u + 1)
                    tt(two, two, bcast(rstd[:, :], 2), ALU.mult).then_inc(qkv_scaled, 1)
                dve.wait_ge(k_gained, g + 1)
                tt(kr[:, :], k_gn[:, :], COS_H, ALU.mult).then_inc(k_cos, 1)
                dve.wait_ge(q_gained, g + 1)
                tt(qr[:, :, :], gated[:, :, :], bcast(COS_H, 4), ALU.mult).then_inc(q_cos, 1)
                dve.wait_ge(k_root, g + 1)
                nc.vector.reciprocal(k_rt[:, :], k_rt[:, :]).then_inc(k_inv, 1)
                tt(k_sq[:, :], ps[:, 6, TOK:], SIN_H, ALU.mult).then_inc(k_sin, 1)
                dve.wait_ge(k_cos, g + 1)
                dve.wait_ge(k_sin, g + 1)
                tt(kr[:, :], kr[:, :], k_sq[:, :], ALU.add).then_inc(k_roped, 1)
                dve.wait_ge(k_roped, g + 1)
                dve.wait_ge(k_inv, g + 1)
                tt(kr[:, :], kr[:, :], k_rt[:, :], ALU.mult).then_inc(k_ready, 1)
                dve.wait_ge(q_root, g + 1)
                tt(sums[:, :, :], ps[:, 0:4, TOK:], bcast(SIN_H, 4), ALU.mult).then_inc(q_sin, 1)
                nc.vector.reciprocal(total[:, :, :], total[:, :, :]).then_inc(q_inv, 1)
                dve.wait_ge(q_cos, g + 1)
                dve.wait_ge(q_sin, g + 1)
                tt(qr[:, :, :], qr[:, :, :], sums[:, :, :], ALU.add).then_inc(q_roped, 1)
                dve.wait_ge(q_roped, g + 1)
                dve.wait_ge(q_inv, g + 1)
                tt(qr[:, :, :], qr[:, :, :], total[:, :, :], ALU.mult).then_inc(q_ready, 1)
                dve.wait_ge(s_made, g + 1)
                dve.wait_ge(mask_ready, 1)
                nc.vector.scalar_tensor_tensor(prob[:, :, :], ps[:, 0:4, 0:384], HD ** -0.5, bcast(mask[:, :], 4),
                                               ALU.mult, ALU.add).then_inc(logit_ready, 1)
                dve.wait_ge(logit_ready, g + 1)
                for a, (c0, c1) in enumerate(COLS):
                    nc.vector.tensor_reduce(peak[:, a, :], prob[:, :, c0:c1], AX_X, ALU.max).then_inc(peak_done, 1)
                dve.wait_ge(peak_done, 2 * g + 2)
                nc.vector.tensor_scalar(npeak[:, :, :], peak[:, :, :], -1.0, None, ALU.mult).then_inc(npeak_done, 1)
                dve.wait_ge(exp_done, 8 * g + 8)
                nc.vector.reciprocal(rden[:, :, :], den[:, :, :]).then_inc(rden_done, 1)
                dve.wait_ge(rden_done, g + 1)
                for a, (c0, c1) in enumerate(COLS):
                    tt(prob[:, :, c0:c1], prob[:, :, c0:c1], per_tile(rden[:, a, :], c1 - c0),
                       ALU.mult).then_inc(prob_ready, 1)
                dve.wait_ge(o_hi, g + 1)
                tiles = bass.ds(4 * g, 4)
                tt(hs[:, tiles, TOK:], ps[:, 4:8, 0:TOK], f32(hs[:, tiles, 0:TOK]),
                   ALU.subtract).then_inc(high_read, 1)

            def gate_sum(fb, done):
                dve.wait_ge(gate_cross, fb + done + 1)
                tt(gated[:, :, :], ps[:, 0:4, 0:TOK], cross[:, :, :], ALU.add).then_inc(gate_summed, 1)

            def gate_scale(fb, done):
                dve.wait_ge(gate_summed, fb + done + 1)
                tt(gated[:, :, :], gated[:, :, :], bcast(rstd[:, :], 4), ALU.mult).then_inc(gate_scaled, 1)

            def up_sum(fb, done):
                dve.wait_ge(up_cross, fb + done + 1)
                tt(total[:, :, :], ps[:, 4:8, 0:TOK], cross[:, :, :], ALU.add).then_inc(up_summed, 1)
                dve.wait_ge(up_summed, fb + done + 1)
                tt(total[:, :, :], total[:, :, :], bcast(rstd[:, :], 4), ALU.mult).then_inc(up_scaled, 1)
                dve.wait_ge(up_scaled, fb + done + 1)
                dve.wait_ge(gate_silu, fb + done + 1)
                tt(total[:, :, :], total[:, :, :], gated[:, :, :], ALU.mult).then_inc(hidden_done, 1)

            def hidden_low(fb, done):
                dve.wait_ge(hidden_hi, fb + done + 1)
                tiles = bass.ds(4 * fb, 4)
                tt(hs[:, tiles, TOK:], total[:, :, :], f32(hs[:, tiles, 0:TOK]), ALU.subtract).then_inc(hidden_ready, 1)

            def gate_steps(fb, done):
                return {11: [lambda: gate_sum(fb, done), lambda: gate_scale(fb, done)]}

            def up_steps(fb, done):
                return {3: [lambda: up_sum(fb, done)], 5: [lambda: hidden_low(fb, done)]}

            def ffn(layer, first, q, before):
                done = FT // 4 * layer
                steps_between(first, 16, before | {10: [lambda: rstd_step(q)]} | gate_steps(0, done))
                with dve.Fori(1, FT // 4) as i:
                    steps_between(first, 16, up_steps(i - 1, done) | gate_steps(i, done), 16, i)
                return up_steps(FT // 4 - 1, done)

            def conv_sum(i, u):
                dst = gated if u == 0 else total
                dve.wait_ge(cv_cross, 3 * i + u + 1)
                tt(dst[:, 0:2, :], ps[:, 2 * u:2 * u + 2, 0:TOK], cross[:, 0:2, :], ALU.add).then_inc(cv_summed, 1)

            def conv_scale(i, u):
                dst = gated if u == 0 else total
                dve.wait_ge(cv_summed, 3 * i + u + 1)
                tt(dst[:, 0:2, :], dst[:, 0:2, :], bcast(rstd[:, :], 2), ALU.mult).then_inc(cv_scaled, 1)

            def conv_z(i):
                dve.wait_ge(cv_scaled, 3 * i + 2)
                if isinstance(i, int):
                    dve.wait_ge(const_set, 2)
                tt(z[:, :, 2:TOK + 2], gated[:, 0:2, :], total[:, 0:2, :], ALU.mult).then_inc(z_ready, 1)

            def conv_taps(i, which):
                dve.wait_ge(z_ready, i + 1)
                for t in which:
                    for m in range(2):
                        tap = taps[:, t, bass.ds(2 * i + m, 1)]
                        src = z[:, m, t:t + TOK]
                        if t == 0:
                            ins = nc.vector.tensor_scalar(ytap[:, m, :], src, tap, None, ALU.mult)
                        else:
                            dve.wait_ge(tap_step, 6 * i + 2 * t + m - 1)
                            ins = nc.vector.scalar_tensor_tensor(ytap[:, m, :], src, tap, ytap[:, m, :],
                                                                 ALU.mult, ALU.add)
                        ins.then_inc(tap_step, 1)

            def conv_gate(i):
                dve.wait_ge(cv_scaled, 3 * i + 3)
                dve.wait_ge(tap_step, 6 * i + 6)
                tt(total[:, 0:2, :], total[:, 0:2, :], ytap[:, :, :], ALU.mult).then_inc(y_done, 1)

            def conv_low(i):
                dve.wait_ge(y_hi, i + 1)
                tiles = bass.ds(2 * i, 2)
                tt(hs[:, tiles, TOK:], total[:, 0:2, :], f32(hs[:, tiles, 0:TOK]), ALU.subtract).then_inc(y_ready, 1)

            def c_steps(i):
                return {7: [lambda: conv_sum(i, 0), lambda: conv_scale(i, 0)]}

            def u_steps(i):
                return {11: [lambda: conv_sum(i, 1), lambda: conv_scale(i, 1), lambda: conv_z(i)]}

            def b_steps(i):
                return {0: [lambda: conv_taps(i, (0, 1))], 1: [lambda: conv_taps(i, (2,))],
                        3: [lambda: conv_sum(i, 2), lambda: conv_scale(i, 2), lambda: conv_gate(i)],
                        5: [lambda: conv_low(i)]}

            def conv(before):
                steps_between(S_CV, 12, before | {7: [lambda: conv_sum(0, 0)],
                                                  10: [lambda: rstd_step(2), lambda: conv_after_stat()]} | u_steps(0))
                with dve.Fori(1, 8) as i:
                    steps_between(S_CV, 12, b_steps(i - 1) | c_steps(i) | u_steps(i), 12, i)
                return b_steps(7)

            def conv_after_stat():
                dve.wait_ge(rstd_ready, 3)
                conv_scale(0, 0)
                nc.vector.memset(z[:, :, 0:2], 0.0).then_inc(const_set, 1)

            before = project(S_AO, 1, KT, {})
            before = ffn(0, S_GU0, 1, before)
            before = project(S_DN0, 2, FT, before)
            before = conv(before)
            before = project(S_CO, 3, KT, before)
            before = ffn(1, S_GU1, 3, before)
            before = project(S_DN1, 4, FT, before)
            for step in before[3]:
                step()
            for j in range(4):
                dve.wait_ge(row_made, j + 1)
                nc.vector.tensor_copy(rows[:, 0, WIDE * j:WIDE * (j + 1)], ps[:, j, :]).then_inc(row_ready, 1)

        @block.gpsimd
        def _(pool):
            pool.memset(eps[:, :], EPS).then_inc(const_set, 1)


def shape_constants():
    tables = np.zeros((P, 4, TOK), np.float32)
    pos = np.arange(TOK, dtype=np.float32)
    for at, dim in ((0, HD), (2, ID)):
        inv = np.float32(1.0) / np.float32(10000.0) ** (np.arange(0, dim, 2, dtype=np.float32) / np.float32(dim))
        angle = (pos[None, :] * inv[:, None]).astype(np.float32).astype(np.float64)
        rows = np.arange(P) % (dim // 2)
        tables[:, at] = np.cos(angle)[rows]
        tables[:, at + 1] = np.sin(angle)[rows]

    def rotation(dim):
        r = np.zeros((P, P), np.float32)
        for m in range(P):
            first = m % dim < dim // 2
            r[m + dim // 2 if first else m - dim // 2, m] = -1.0 if first else 1.0
        return r

    dup = np.zeros((P, P), np.float32)
    for m in range(P):
        dup[m % ID, m] = 1.0
    dup_rot = np.zeros((P, P), np.float32)
    rot = rotation(ID)
    for m in range(P):
        dup_rot[:ID, m] = rot[:ID, m % ID]
    mats = np.stack([np.eye(P, dtype=np.float32), np.full((P, P), 1.0 / D, np.float32),
                     np.full((P, P), 1.0 / HD, np.float32), rotation(HD), rotation(ID), dup, dup_rot], axis=1)
    bounds = np.zeros((P, 2, 384), np.float32)
    for a, (c0, c1) in enumerate(COLS):
        query = a * P + np.arange(P)[:, None]
        key = np.arange(c1 - c0)[None, :]
        bounds[:, 0, c0:c1] = np.where(key <= query, np.float32(-FILL), np.float32(FILL))
        bounds[:, 1, c0:c1] = np.where(key <= query, np.float32(0.0), np.float32(DROP))
    return tables, np.ascontiguousarray(mats), bounds


def kernel(x, attn_norm, attn_w_in, attn_q_norm, attn_k_norm, attn_w_out, conv_norm, conv_w_in, conv_w,
           conv_w_out, ffn_norm, ffn_w_gate, ffn_w_up, ffn_w_down):
    import concourse.bacc as bacc
    from concourse.bass_utils import run_bass_kernel_spmd

    def by_partition(a):
        a = np.asarray(a).reshape(-1, KT, P)
        return np.ascontiguousarray(a.transpose(2, 0, 1))

    x, attn_norm, conv_norm, ffn_norm = (np.asarray(a) for a in (x, attn_norm, conv_norm, ffn_norm))
    tables, mats, bounds = shape_constants()
    arrays = {
        "x": x[0],
        "attn_w_in": attn_w_in[0], "attn_w_out": attn_w_out[0],
        "conv_w_in": conv_w_in[0], "conv_w_out": conv_w_out[0],
        "w_gate": ffn_w_gate, "w_up": ffn_w_up, "w_down": ffn_w_down,
        "gains": by_partition(np.stack([attn_norm[0], ffn_norm[0], conv_norm[0], ffn_norm[1]])),
        "head_gains": np.stack([np.asarray(attn_q_norm)[0], np.asarray(attn_k_norm)[0]], axis=1),
        "conv_taps": by_partition(np.asarray(conv_w)[0]),
        "tables": tables, "mats": mats, "bounds": bounds,
    }
    arrays = {f"in_{k}": np.ascontiguousarray(v) for k, v in arrays.items()}
    nc = bacc.Bacc("TRN2", target_bir_lowering=False, num_devices=1)
    args = [nc.dram_tensor(k, v.shape, mybir.dt.from_np(v.dtype), kind="ExternalInput").ap() for k, v in arrays.items()]
    out = nc.dram_tensor("out", (TOK, D), F32, kind="ExternalOutput").ap()
    trunk(nc, *args, out)
    r = run_bass_kernel_spmd(nc, [arrays], core_ids=[0])
    return np.asarray(r.results[0]["out"]).reshape(1, TOK, D)
```

```python
from contextlib import ExitStack

import numpy as np

import concourse.bass as bass
from concourse import mybir
from concourse.alu_op_type import AluOpType as ALU

ACT = mybir.ActivationFunctionType
F32 = mybir.dt.float32
F32R = mybir.dt.float32r
AX_X = mybir.AxisListType.X

P = 128
TOK = 256
D = 2048
KT = D // P
HEADS, KV, REP, HD = 16, 4, 4, 128
IH, ID = 16, 64
F = 5632
FT = F // P
TOPK = 64
EPS = 1e-6
RING = 4
SLOT = 1024
WIDE, NARROW = 512, 256
COLS = ((0, 128), (128, 384))
FILL = -3.0e38
TAKEN = -3.3e38
DROP = -1.0e30

S_KI = 0
S_QI = S_KI + 4
S_QKV = S_QI + 4 * 4
S_AO = S_QKV + KV * 12
S_GU0 = S_AO + 4 * 8
S_DN0 = S_GU0 + (FT // 4) * 16
S_CV = S_DN0 + 4 * 22
S_CO = S_CV + 8 * 12
S_GU1 = S_CO + 4 * 8
S_DN1 = S_GU1 + (FT // 4) * 16
S_END = S_DN1 + 4 * 22


def trunk(nc, x, attn_w_in, attn_w_out, conv_w_in, conv_w_out, w_gate, w_up, w_down,
          gains, head_gains, conv_taps, tables, mats, bounds, out):
    with ExitStack() as ctx:
        def sb(name, shape, dt=F32, stack=ctx):
            return stack.enter_context(nc.sbuf_tensor(name, shape, dt))

        def sem(name):
            return ctx.enter_context(nc.semaphore(name))

        stage = sb("stage", [P, RING, SLOT])
        w_hi = sb("w_hi", [P, RING, SLOT], F32R)
        w_lo = sb("w_lo", [P, RING, SLOT], F32R)
        xs = sb("xs", [P, KT, 2 * TOK], F32R)
        res = sb("res", [P, KT, TOK])
        gain = sb("gain", [P, 4, KT])
        hgain = sb("hgain", [P, 2])
        taps = sb("taps", [P, 3, KT])
        mat = sb("mat", [P, 2, P])
        cross = sb("cross", [P, 4, TOK])
        total = sb("total", [P, 4, TOK])
        gated = sb("gated", [P, 4, TOK])
        square = sb("square", [P, 4, TOK])
        sums = sb("sums", [P, 4, TOK])
        colsum = sb("colsum", [P, TOK])
        rstd = sb("rstd", [P, TOK])
        eps = sb("eps", [P, 2])

        part = ExitStack()
        sb("head_outputs", [P, KT, 2 * TOK], F32R, stack=part)
        tab = sb("tab", [P, 4, TOK], stack=part)
        mat_a = sb("mat_a", [P, 5, P], stack=part)
        bound = sb("bound", [P, 2, 384], stack=part)
        kiwi = sb("kiwi", [P, TOK], stack=part)
        kir = sb("kir", [P, TOK], stack=part)
        qir = sb("qir", [P, 2, TOK], stack=part)
        wt = sb("wt", [P, 2, IH], stack=part)
        score = sb("score", [P, 384], stack=part)
        top8 = sb("top8", [P, 8, 2, 8], stack=part)
        mask = sb("mask", [P, 384], stack=part)
        raw = sb("raw", [P, 6, TOK], stack=part)
        k_sq = sb("k_sq", [P, TOK], stack=part)
        k_gn = sb("k_gn", [P, TOK], stack=part)
        k_rt = sb("k_rt", [P, TOK], stack=part)
        kr = sb("kr", [P, TOK], stack=part)
        qr = sb("qr", [P, 4, TOK], stack=part)
        vt = sb("vt", [P, 2, HD], stack=part)
        q_rt = sb("q_rt", [P, 2, 4], stack=part)
        peak = sb("peak", [P, 2, 4], stack=part)
        npeak = sb("npeak", [P, 2, 4], stack=part)
        den = sb("den", [P, 2, 4], stack=part)
        rden = sb("rden", [P, 2, 4], stack=part)
        early = ExitStack()
        xin = sb("xin", [P, 2, D], stack=early)
        early.close()
        late = ExitStack()
        prob = sb("prob", [P, 1536], stack=late)
        pt = sb("pt", [P, 1536], stack=late)
        late.close()
        part.close()
        whole = ExitStack()
        hs = sb("hs", [P, FT, 2 * TOK], F32R, stack=whole)
        whole.close()
        rows = sb("rows", [P, 2, D])

        rms = colsum
        ytap = square[:, 0:2, :]
        z = sums[:, :, :].rearrange("p m t -> p (m t)")[:, 0:2 * (TOK + 2)].rearrange("p (m t) -> p m t", m=2)

        def f32(ap):
            return ap.bitcast(F32)

        ps = ctx.enter_context(nc.psum_tensor("ps", [P, 8, 512], F32))
        ps_heads = ps[:, 4:7, :].rearrange("p b c -> p (b c)")

        IDENT, MEAN_D = (mat[:, i, :] for i in range(2))
        MEAN_H, ROT_H, ROT_I, DUP, DUP_ROT = (mat_a[:, i, :] for i in range(5))

        in_ident = sem("in_ident")
        in_x = [sem(f"in_x{j}") for j in range(4)]
        in_gain = sem("in_gain")
        in_small = sem("in_small")
        loaded = [sem(f"loaded{i}") for i in range(RING)]
        v_loaded = [sem(f"v_loaded{i}") for i in range(RING)]
        hi_done = sem("hi_done")
        lo_done = sem("lo_done")
        slot_used = sem("slot_used")
        const_set = sem("const_set")
        x_turned = sem("x_turned")
        res_cross = sem("res_cross")
        res_summed = sem("res_summed")
        res_added = sem("res_added")
        res_squared = sem("res_squared")
        res_gained = sem("res_gained")
        res_hi = sem("res_hi")
        xs_ready = sem("xs_ready")
        sums_done = sem("sums_done")
        stat_sum = sem("stat_sum")
        stat_made = sem("stat_made")
        stat_root = sem("stat_root")
        rstd_ready = sem("rstd_ready")
        ki_scaled = sem("ki_scaled")
        ki_turned = sem("ki_turned")
        ki_cross = sem("ki_cross")
        ki_cos = sem("ki_cos")
        ki_sin = sem("ki_sin")
        ki_ready = sem("ki_ready")
        wt_ready = sem("wt_ready")
        qi_cross = sem("qi_cross")
        qi_summed = sem("qi_summed")
        qi_scaled = sem("qi_scaled")
        qi_turned = sem("qi_turned")
        qi_cos = sem("qi_cos")
        qi_sin = sem("qi_sin")
        qi_ready = sem("qi_ready")
        score_made = sem("score_made")
        rel_done = sem("rel_done")
        score_step = sem("score_step")
        top_step = sem("top_step")
        mask_ready = sem("mask_ready")
        qkv_cross = sem("qkv_cross")
        qkv_summed = sem("qkv_summed")
        qkv_scaled = sem("qkv_scaled")
        k_squared = sem("k_squared")
        k_gained = sem("k_gained")
        k_made = sem("k_made")
        k_root = sem("k_root")
        k_inv = sem("k_inv")
        k_cos = sem("k_cos")
        k_sin = sem("k_sin")
        k_roped = sem("k_roped")
        k_ready = sem("k_ready")
        v_made = sem("v_made")
        v_ready = sem("v_ready")
        q_squared = sem("q_squared")
        q_gained = sem("q_gained")
        q_turned = sem("q_turned")
        q_var = sem("q_var")
        q_root = sem("q_root")
        q_inv = sem("q_inv")
        q_cos = sem("q_cos")
        q_sin = sem("q_sin")
        q_ready = sem("q_ready")
        s_made = sem("s_made")
        logit_ready = sem("logit_ready")
        peak_done = sem("peak_done")
        npeak_done = sem("npeak_done")
        exp_done = sem("exp_done")
        rden_done = sem("rden_done")
        prob_ready = sem("prob_ready")
        pt_made = sem("pt_made")
        pt_copied = sem("pt_copied")
        o_made = sem("o_made")
        o_hi = sem("o_hi")
        o_read = sem("o_read")
        gate_cross = sem("gate_cross")
        gate_summed = sem("gate_summed")
        gate_scaled = sem("gate_scaled")
        gate_silu = sem("gate_silu")
        up_cross = sem("up_cross")
        up_summed = sem("up_summed")
        up_scaled = sem("up_scaled")
        hidden_done = sem("hidden_done")
        hidden_hi = sem("hidden_hi")
        hidden_ready = sem("hidden_ready")
        cv_cross = sem("cv_cross")
        cv_summed = sem("cv_summed")
        cv_scaled = sem("cv_scaled")
        zeros_set = sem("zeros_set")
        z_ready = sem("z_ready")
        tap_step = sem("tap_step")
        y_done = sem("y_done")
        y_hi = sem("y_hi")
        y_ready = sem("y_ready")
        row_made = sem("row_made")
        row_ready = sem("row_ready")
        row_ready_act = sem("row_ready_act")
        stored = sem("stored")

        def bcast(ap, tiles):
            return ap.unsqueeze(1).to_broadcast([P, tiles, ap.shape[1]])

        def per_tile(ap, width):
            return ap.unsqueeze(2).to_broadcast([P, ap.shape[1], width])

        index_scores = prob[:, :].rearrange("p (h c) -> p h c", h=4)

        def chunk(a, h):
            return slice(P * h, P * (h + 1)) if a == 0 else slice(512 + TOK * h, 512 + TOK * (h + 1))

        def heads(ap, a):
            return (ap[:, 0:512] if a == 0 else ap[:, 512:1536]).rearrange("p (h c) -> p h c", h=4)

        def by_query_tile(ap):
            return ap.rearrange("p h (a q) -> p a h q", a=2)

        def merged(*steps):
            out = {}
            for part_steps in steps:
                for at, some in part_steps.items():
                    out[at] = out.get(at, []) + some
            return out

        STREAM_BANKS = ((0, 2), (2, 4), (0, 2))
        QI_BANKS = ((0, 2), (2, 4))
        INDEX_SLOTS = 16

        block = ctx.enter_context(nc.Block())

        @block.sync
        def _(sp):
            def load(n, pos, rows_of, width):
                k = rows_of.shape[0] // P
                if not isinstance(n, int) or n >= RING:
                    sp.wait_ge(lo_done, n - (RING - 1))
                dst = stage[:, pos, 0:k * width].rearrange("p (k n) -> p k n", k=k)
                sp.dma_start(dst, rows_of.rearrange("(k p) n -> p k n", p=P)).then_inc(loaded[pos], 16)

            def load_block(n, w, base, col, width, tiles):
                per = SLOT // width if width >= NARROW else 4
                for s in range(tiles // per):
                    load(n + s, s % RING, w[s * per * P:(s + 1) * per * P, base:][:, bass.ds(col, width)], width)

            def load_x(j):
                sp.dma_start(xin[:, :, WIDE * j:WIDE * (j + 1)],
                             x[:, WIDE * j:WIDE * (j + 1)].rearrange("(a p) n -> p a n", p=P)).then_inc(in_x[j], 16)

            sp.dma_start(mat.ap(), mats[:, 0:2, :]).then_inc(in_ident, 16)
            load_x(0)
            load_x(1)
            w_in = attn_w_in
            load_block(S_KI, w_in, D + 2 * KV * HD + IH * ID, 0, ID + IH, KT)
            load_x(2)
            load_x(3)
            with sp.Fori(0, 4) as i:
                load_block(S_QI + 4 * i, w_in, D + 2 * KV * HD, NARROW * i, NARROW, KT)
            with sp.Fori(0, KV) as g:
                n = S_QKV + 12 * g
                for s in range(4):
                    rows4 = slice(s * 4 * P, (s + 1) * 4 * P)
                    sp.wait_ge(lo_done, n + s - (RING - 1))
                    dst = stage[:, s, :].rearrange("p (k n) -> p k n", k=4)
                    for side, arrived in ((0, loaded[s]), (1, v_loaded[s])):
                        src = w_in[rows4, D + side * KV * HD:][:, bass.ds(HD * g, HD)]
                        sp.dma_start(dst[:, :, side * HD:(side + 1) * HD],
                                     src.rearrange("(k p) n -> p k n", p=P)).then_inc(arrived, 16)
                load_block(n + 4, w_in, 0, WIDE * g, NARROW, KT)
                load_block(n + 8, w_in, NARROW, WIDE * g, NARROW, KT)

            def load_wide(first, w, tiles):
                slots = tiles // 2
                with sp.Fori(0, 2) as i:
                    for u in range(2):
                        for s in range(slots):
                            load(first + 2 * slots * i + u * slots + s, (u * slots + s) % RING,
                                 w[s * 2 * P:(s + 1) * 2 * P, WIDE * u:][:, bass.ds(2 * WIDE * i, WIDE)], WIDE)

            def load_ffn(first, layer):
                with sp.Fori(0, FT // 4) as i:
                    load_block(first + 16 * i, w_gate[layer], 0, WIDE * i, WIDE, KT)
                    load_block(first + 16 * i + 8, w_up[layer], 0, WIDE * i, WIDE, KT)

            load_wide(S_AO, attn_w_out, KT)
            load_ffn(S_GU0, 0)
            load_wide(S_DN0, w_down[0], FT)
            with sp.Fori(0, 8) as i:
                for u, base in enumerate((D, 2 * D, 0)):
                    col = NARROW * i if u < 2 else (P * i) * 2
                    load_block(S_CV + 12 * i + 4 * u, conv_w_in, base, col, NARROW, KT)
            load_wide(S_CO, conv_w_out, KT)
            load_ffn(S_GU1, 1)
            load_wide(S_DN1, w_down[1], FT)

            for a in range(2):
                sp.wait_ge(row_ready if a == 0 else row_ready_act, 4)
                sp.dma_start(out[a * P:(a + 1) * P, :], rows[:, a, :]).then_inc(stored, 16)
            sp.wait_ge(stored, 32)

        @block.tensor
        def _(pe):
            def stream(n, banks, width, tiles, moving, ready=None, count=P, place=0, after=None):
                per = SLOT // width if width >= NARROW else 4
                step = width if width >= NARROW else count
                for s in range(tiles // per):
                    pe.wait_ge(lo_done, n + s + 1)
                    for kk in range(per):
                        k = s * per + kk
                        if ready is not None:
                            ready(k)
                        rhs = moving(k)
                        for m in range((width + P - 1) // P):
                            at = slice(kk * step + m * P, kk * step + m * P + count)
                            bank = ps[0:count, banks[m], :]
                            slot = (place + s) % RING
                            full = (bank, w_hi[:, slot, at], rhs)
                            low = (bank[:, TOK:], w_lo[:, slot, at], rhs[:, 0:TOK])
                            last = k == tiles - 1
                            if last:
                                pe.matmul(*low, start=False, stop=False)
                                mm = pe.matmul(*full, start=False, stop=True)
                            else:
                                pe.matmul(*full, start=k == 0, stop=False)
                                mm = pe.matmul(*low, start=False, stop=False)
                    mm.then_inc(slot_used, 1)
                    for other in (after or {}).get(s, ()):
                        other()

            low_banks, high_banks = (0, 1, 2, 3), (4, 5, 6, 7)

            def xs_tile(k):
                return xs[:, k, :]

            def hs_tile(k):
                return hs[:, k, :]

            def xs_wait(stage_no):
                def ready(k):
                    if k % 4 == 0:
                        pe.wait_ge(xs_ready, 4 * stage_no + k // 4 + 1)
                return ready

            def stat(no):
                pe.wait_ge(stat_sum, no + 1)
                pe.matmul(ps[:, 7, 0:TOK], MEAN_D, colsum[:, :], start=True, stop=True).then_inc(stat_made, 1)

            pe.wait_ge(in_ident, 16)
            for j in range(4):
                pe.wait_ge(in_x[j], 16)
                if j >= 2:
                    pe.wait_ge(res_added, j - 1)
                for m in range(4):
                    for a in range(2):
                        mm = pe.transpose(ps[:, 4 * (j % 2) + m, a * P:(a + 1) * P],
                                          xin[:, a, (4 * j + m) * P:(4 * j + m + 1) * P], IDENT)
                mm.then_inc(x_turned, 1)

            def ki_turn():
                pe.wait_ge(ki_scaled, 1)
                pe.wait_ge(in_small, 80)
                pe.matmul(ps[:, 6, 0:TOK], DUP[0:ID, :], kiwi[0:ID, :], start=True, stop=True)
                pe.matmul(ps[:, 6, TOK:], DUP_ROT[0:ID, :], kiwi[0:ID, :], start=True, stop=True)
                pe.wait_ge(stat_root, 1)
                for a in range(2):
                    mm = pe.transpose(ps[:, 7, a * P:a * P + 80], kiwi[0:80, a * P:(a + 1) * P], IDENT[0:80, 0:80])
                mm.then_inc(ki_turned, 1)

            def qi_turn(i):
                pe.wait_ge(qi_scaled, i + 1)
                if i:
                    pe.wait_ge(rel_done, i)
                else:
                    pe.wait_ge(wt_ready, 1)
                for m in range(2):
                    mm = pe.matmul(ps[:, 7, m * TOK:(m + 1) * TOK], ROT_I, total[:, m, :], start=True, stop=True)
                mm.then_inc(qi_turned, 1)

            def score_heads(i):
                pe.wait_ge(qi_ready, i + 1)
                if i == 0:
                    pe.wait_ge(ki_ready, 1)
                for h in range(4):
                    half = slice(ID * (h % 2), ID * (h % 2) + ID)
                    for a, (c0, c1) in enumerate(COLS):
                        mm = pe.matmul(ps[:, 4 + h, c0:c1], qir[half, h // 2, a * P:(a + 1) * P],
                                       kir[half, 0:c1 - c0], start=True, stop=True)
                mm.then_inc(score_made, 1)

            pe.wait_ge(res_added, 3)
            stream(S_KI, (2,), ID + IH, KT, xs_tile, xs_wait(0), count=ID + IH)
            pe.wait_ge(res_added, 4)
            stream(S_QI, (0, 1), NARROW, KT, xs_tile, after={0: [lambda: stat(0)], 3: [ki_turn]})
            pe.wait_ge(qi_summed, 1)
            stream(S_QI + 4, (2, 3), NARROW, KT, xs_tile, after={2: [lambda: qi_turn(0)]})
            pe.wait_ge(qi_summed, 2)
            stream(S_QI + 8, (0, 1), NARROW, KT, xs_tile,
                   after={0: [lambda: score_heads(0)], 2: [lambda: qi_turn(1)]})
            pe.wait_ge(qi_summed, 3)
            stream(S_QI + 12, (2, 3), NARROW, KT, xs_tile,
                   after={0: [lambda: score_heads(1)], 2: [lambda: qi_turn(2)]})

            def turn_kvq(g):
                pe.wait_ge(k_squared, g + 1)
                pe.matmul(ps[:, 4, 0:TOK], MEAN_H, k_sq[:, :], start=True, stop=True)
                pe.wait_ge(k_gained, g + 1)
                pe.matmul(ps[:, 4, TOK:], ROT_H, k_gn[:, :], start=True, stop=True).then_inc(k_made, 1)
                for a in range(2):
                    mm = pe.transpose(ps[:, 5, a * P:(a + 1) * P], raw[:, 1, a * P:(a + 1) * P], IDENT)
                mm.then_inc(v_made, 1)
                pe.wait_ge(q_gained, 2 * g + 1)
                for m in range(2):
                    mm = pe.matmul(ps[:, 6, m * TOK:(m + 1) * TOK], ROT_H, gated[:, m, :], start=True, stop=True)
                mm.then_inc(q_turned, 1)

            def turn_q23(p):
                pe.wait_ge(q_gained, 2 * p + 2)
                for m in range(2):
                    mm = pe.matmul(ps[:, 7, m * TOK:(m + 1) * TOK], ROT_H, gated[:, 2 + m, :], start=True, stop=True)
                mm.then_inc(q_turned, 1)

            def vars_q(p):
                pe.wait_ge(q_squared, 2 * p + 2)
                pe.wait_ge(k_sin, p + 1)
                for a in range(2):
                    for h in range(REP):
                        mm = pe.matmul(ps[:, 4, 4 * a + h:4 * a + h + 1], square[:, h, a * P:(a + 1) * P],
                                       MEAN_H[:, 0:1], start=True, stop=True)
                mm.then_inc(q_var, 1)

            def logits(p):
                pe.wait_ge(k_ready, p + 1)
                pe.wait_ge(q_ready, p + 1)
                pe.wait_ge(q_root, p + 1)
                pe.wait_ge(v_ready, p + 1)
                for h in range(REP):
                    for a, (c0, c1) in enumerate(COLS):
                        mm = pe.matmul(ps_heads[:, chunk(a, h)], qr[:, h, a * P:(a + 1) * P], kr[:, 0:c1 - c0],
                                       start=True, stop=True)
                mm.then_inc(s_made, 1)

            def turn_prob(p):
                pe.wait_ge(prob_ready, 2 * p + 2)
                for c in range(12):
                    mm = pe.transpose(ps_heads[:, c * P:(c + 1) * P], prob[:, c * P:(c + 1) * P], IDENT)
                mm.then_inc(pt_made, 1)

            def outputs(p):
                pe.wait_ge(pt_copied, p + 1)
                pe.matmul(ps[:, 4, :], vt[:, 0, :], pt[:, 0:512], start=True, stop=True)
                later = heads(pt, 1)
                pe.matmul(ps[:, 5, :].rearrange("p (h q) -> p h q", h=4), vt[:, 0, :], later[:, :, 0:P],
                          start=True, stop=False)
                pe.matmul(ps[:, 5, :].rearrange("p (h q) -> p h q", h=4), vt[:, 1, :], later[:, :, P:],
                          start=False, stop=True).then_inc(o_made, 1)

            def group(g, p, after_kv, after_q01, after_q23):
                n = S_QKV + 12 * g
                if p is None:
                    pe.wait_ge(qi_summed, 4)
                else:
                    pe.wait_ge(qkv_summed, 3 * g)
                stream(n, (0, 1), NARROW, KT, xs_tile, after=after_kv)
                if p is None:
                    pe.wait_ge(qi_summed, 5)
                stream(n + 4, (2, 3), NARROW, KT, xs_tile, after=after_q01)
                pe.wait_ge(qkv_summed, 3 * g + 1)
                stream(n + 8, (0, 1), NARROW, KT, xs_tile, after=after_q23)
                if p is None:
                    pe.wait_ge(rel_done, 4)
                else:
                    pe.wait_ge(o_read, g)
                turn_kvq(g)

            group(0, None, {0: [lambda: score_heads(2)], 2: [lambda: qi_turn(3)]},
                  {0: [lambda: score_heads(3)]}, {})
            with pe.Fori(1, KV) as g:
                group(g, g - 1, {1: [lambda: turn_q23(g - 1), lambda: vars_q(g - 1)], 3: [lambda: logits(g - 1)]},
                      {}, {0: [lambda: turn_prob(g - 1)], 1: [lambda: outputs(g - 1)]})

            def ao_ready(k):
                if k in (0, KT - REP):
                    pe.wait_ge(o_read, KV if k else KV - 1)
            last = KV - 1
            for j in range(4):
                if j == 0:
                    pe.wait_ge(qkv_summed, 3 * KV)
                elif j == 1:
                    pe.wait_ge(o_read, KV)
                else:
                    pe.wait_ge(res_added, 3 + j)
                stream(S_AO + 8 * j, (low_banks, high_banks)[j % 2], WIDE, KT, hs_tile, None if j else ao_ready,
                       after=None if j else {1: [lambda: turn_q23(last), lambda: vars_q(last)],
                                             3: [lambda: logits(last)],
                                             5: [lambda: turn_prob(last), lambda: outputs(last)]})

            def project(first, q, tiles, waits, ready=None):
                slots = tiles // 2
                with pe.Fori(0, 2) as i:
                    for u in range(2):
                        waits(u)
                        pe.wait_ge(res_added, 4 * q + 2 * i + u - 1)
                        stream(first + 2 * slots * i + slots * u, (low_banks, high_banks)[u], WIDE, tiles,
                               hs_tile, ready, place=slots * u % RING)

            def ffn(layer, first, q):
                def body(i, first_time):
                    fb = (FT // 4) * layer + i
                    if first_time:
                        pe.wait_ge(res_summed, 4 * (q - 1) + 3)
                    else:
                        pe.wait_ge(gate_summed, fb)
                    stream(first + 16 * i, low_banks, WIDE, KT, xs_tile, xs_wait(q) if first_time else None)
                    if first_time:
                        stat(q)
                        pe.wait_ge(stat_root, q + 1)
                    else:
                        pe.wait_ge(up_summed, fb)
                    stream(first + 16 * i + 8, high_banks, WIDE, KT, xs_tile)
                body(0, True)
                with pe.Fori(1, FT // 4) as i:
                    body(i, False)

            def down(layer, first, q):
                blocks = (FT // 4) * (layer + 1)

                def waits(u):
                    pe.wait_ge(up_summed if u else gate_summed, blocks)

                def ready(k):
                    if k in (0, FT - 4):
                        pe.wait_ge(hidden_ready, blocks if k else blocks - 1)
                project(first, q, FT, waits, ready)

            ffn(0, S_GU0, 1)
            down(0, S_DN0, 2)

            def conv(i, first_time):
                n = S_CV + 12 * i
                if first_time:
                    pe.wait_ge(res_summed, 7)
                else:
                    pe.wait_ge(cv_summed, 3 * i - 2)
                stream(n, (0, 1), NARROW, KT, xs_tile, xs_wait(2) if first_time else None)
                if not first_time:
                    pe.wait_ge(cv_summed, 3 * i - 1)
                stream(n + 4, (2, 3), NARROW, KT, xs_tile)
                if first_time:
                    stat(2)
                else:
                    pe.wait_ge(cv_summed, 3 * i)
                stream(n + 8, (4, 5), NARROW, KT, xs_tile)
            conv(0, True)
            with pe.Fori(1, 8) as i:
                conv(i, False)

            def co_waits(u):
                pe.wait_ge(cv_summed, 23 + u)

            def y_wait(k):
                if k in (0, KT - 2):
                    pe.wait_ge(y_ready, 8 if k else 7)

            project(S_CO, 3, KT, co_waits, y_wait)
            ffn(1, S_GU1, 3)
            down(1, S_DN1, 4)

            pe.wait_ge(res_added, 20)
            for a in range(2):
                for j in range(4):
                    for m in range(4):
                        mm = pe.transpose(ps[:, 4 * a + j, m * P:(m + 1) * P],
                                          res[:, 4 * j + m, a * P:(a + 1) * P], IDENT)
                    mm.then_inc(row_made, 1)

        @block.scalar
        def _(act):
            def split(first, slots, per_loop=0, i=0, at=0):
                for j in range(at, at + slots):
                    n = first + per_loop * i + j
                    act.wait_ge(loaded[j % RING], 16 * ((first + j) // RING + 1) + 16 * (per_loop // RING) * i)
                    if first + j >= RING:
                        act.wait_ge(slot_used, n - (RING - 1))
                    nc.scalar.activation(w_hi[:, j % RING, :], stage[:, j % RING, :], ACT.Copy).then_inc(hi_done, 1)

            def take_cross(banks, dst, n_done, sem_out, count=P):
                act.wait_ge(slot_used, n_done)
                b0, b1 = banks
                nc.scalar.activation(dst, ps[0:count, b0:b1, TOK:], ACT.Copy).then_inc(sem_out, 1)

            def stat(no):
                act.wait_ge(stat_made, no + 1)
                act.wait_ge(const_set, 2)
                nc.scalar.activation(rms[:, :], ps[:, 7, 0:TOK], ACT.Sqrt, bias=eps[:, 0:1]).then_inc(stat_root, 1)

            def res_square(rb):
                act.wait_ge(res_added, rb + 1)
                if not isinstance(rb, int) or rb:
                    act.wait_ge(sums_done, rb)
                j4 = 4 * (rb % 4)
                nc.scalar.activation(square[:, :, :], res[:, j4:j4 + 4, :], ACT.Square).then_inc(res_squared, 1)

            def res_high(rb):
                act.wait_ge(res_gained, rb + 1)
                j4 = 4 * (rb % 4)
                nc.scalar.activation(xs[:, j4:j4 + 4, 0:TOK], gated[:, :, :], ACT.Copy).then_inc(res_hi, 1)

            def steps_between(first, slots, steps, per_loop=0, i=0, at=0):
                for j in range(slots):
                    split(first, 1, per_loop, i, at + j)
                    for step in steps.get(j, ()):
                        step()

            act.dma_start(gain.ap(), gains).then_inc(in_gain, 16)
            for dst, src in ((tab, tables), (mat_a, mats[:, 2:7, :]), (bound, bounds), (hgain, head_gains),
                             (taps, conv_taps)):
                act.dma_start(dst.ap(), src).then_inc(in_small, 16)

            for j in range(4):
                act.wait_ge(x_turned, j + 1)
                b = 4 * (j % 2)
                nc.scalar.activation(res[:, 4 * j:4 * j + 4, :], ps[:, b:b + 4, 0:TOK], ACT.Copy).then_inc(res_added, 1)
                res_square(j)
                res_high(j)
                for s in ((), (0,), (1,), (2, 3))[j]:
                    act.wait_ge(loaded[s], 16)
                    nc.scalar.activation(w_hi[:, s, 0:320], stage[:, s, 0:320], ACT.Copy).then_inc(hi_done, 1)

            def ki_halves():
                act.wait_ge(slot_used, S_QI)
                nc.scalar.activation(cross[0:80, 0, :], ps[0:80, 2, TOK:], ACT.Copy).then_inc(ki_cross, 1)

            def weights_of_heads():
                act.wait_ge(ki_turned, 1)
                nc.scalar.activation(wt[:, :, :], ps[:, 7, 0:TOK].rearrange("p (a c) -> p a c", a=2)[:, :, ID:ID + IH],
                                     ACT.Copy, scale=IH ** -0.5 * ID ** -0.5).then_inc(wt_ready, 1)

            def qi_halves(i):
                act.wait_ge(qi_summed, i + 1)
                take_cross(QI_BANKS[i % 2], cross[:, 0:2, :], S_QI + 4 * i + 4, qi_cross)

            def relu(i):
                act.wait_ge(score_made, i + 1)
                act.wait_ge(score_step, 8 * i + 1)
                nc.scalar.activation(index_scores[:, :, :], ps[:, 4:8, 0:384], ACT.Relu).then_inc(rel_done, 1)

            def qkv_halves(g, u):
                if u == 0 and isinstance(g, int):
                    act.wait_ge(qi_summed, 5)
                else:
                    act.wait_ge(qkv_summed, 3 * g + u)
                take_cross(STREAM_BANKS[u], cross[:, 0:2, :], S_QKV + 12 * g + 4 * u + 4, qkv_cross)

            def gain_k(g):
                act.wait_ge(qkv_scaled, 3 * g + 1)
                if isinstance(g, int):
                    act.wait_ge(ki_ready, 1)
                    act.wait_ge(in_small, 80)
                else:
                    act.wait_ge(k_roped, g)
                nc.scalar.activation(k_sq[:, :], raw[:, 0, :], ACT.Square).then_inc(k_squared, 1)
                nc.scalar.activation(k_gn[:, :], raw[:, 0, :], ACT.Copy, scale=hgain[:, 1:2]).then_inc(k_gained, 1)

            def gain_q(g, u):
                act.wait_ge(qkv_scaled, 3 * g + 2 + u)
                if u == 0 and isinstance(g, int):
                    act.wait_ge(qi_ready, 4)
                elif not isinstance(g, int) or g:
                    act.wait_ge(q_cos, g)
                    act.wait_ge(q_var, g)
                nc.scalar.activation(square[:, 2 * u:2 * u + 2, :], raw[:, 2 + 2 * u:4 + 2 * u, :],
                                     ACT.Square).then_inc(q_squared, 1)
                nc.scalar.activation(gated[:, 2 * u:2 * u + 2, :], raw[:, 2 + 2 * u:4 + 2 * u, :], ACT.Copy,
                                     scale=hgain[:, 0:1]).then_inc(q_gained, 1)

            def root_k(p):
                act.wait_ge(k_made, p + 1)
                nc.scalar.activation(k_rt[:, :], ps[:, 4, 0:TOK], ACT.Sqrt, bias=eps[:, 0:1]).then_inc(k_root, 1)

            def values(p):
                act.wait_ge(v_made, p + 1)
                nc.scalar.activation(vt[:, :, :], ps[:, 5, 0:TOK].rearrange("p (a c) -> p a c", a=2),
                                     ACT.Copy).then_inc(v_ready, 1)

            def root_q(p):
                act.wait_ge(q_var, p + 1)
                nc.scalar.activation(q_rt[:, :, :], ps[:, 4, 0:8].rearrange("p (a h) -> p a h", a=2), ACT.Sqrt,
                                     bias=eps[:, 1:2], scale=float(HD)).then_inc(q_root, 1)

            def exps(p):
                act.wait_ge(npeak_done, p + 1)
                for h in range(REP):
                    for a in range(2):
                        nc.scalar.activation(prob[:, chunk(a, h)], prob[:, chunk(a, h)], ACT.Exp,
                                             bias=npeak[:, a, h:h + 1],
                                             accum_out=den[:, a, h:h + 1]).then_inc(exp_done, 1)

            def copy_pt(p):
                act.wait_ge(pt_made, p + 1)
                nc.scalar.activation(pt[:, :], ps_heads, ACT.Copy).then_inc(pt_copied, 1)

            def out_high(p):
                act.wait_ge(o_made, p + 1)
                nc.scalar.activation(by_query_tile(hs[:, bass.ds(4 * p, 4), 0:TOK]),
                                     ps[:, 4:6, :].rearrange("p a (h q) -> p a h q", h=4), ACT.Copy).then_inc(o_hi, 1)

            def kv_q01_steps(g):
                return {7: [lambda: qkv_halves(g, 0)],
                        11: [lambda: qkv_halves(g, 1), lambda: gain_k(g), lambda: gain_q(g, 0)]}

            def head_steps(p, at_exp, at_out):
                return merged({2: [lambda: qkv_halves(p, 2)],
                               3: [lambda: root_k(p), lambda: gain_q(p, 1), lambda: values(p)],
                               5: [lambda: root_q(p)]},
                              {at_exp: [lambda: exps(p)]},
                              {at_out: [lambda: copy_pt(p)]})

            def group(g, steps):
                for j in range(12):
                    if j < RING:
                        act.wait_ge(v_loaded[j], 16 * g + 16)
                    split(S_QKV, 1, 12, g, j)
                    for step in steps.get(j, ()):
                        step()

            index_steps = {3: [ki_halves], 4: [lambda: stat(0)], 7: [lambda: qi_halves(0), weights_of_heads],
                           11: [lambda: qi_halves(1)], 12: [lambda: relu(0)], 15: [lambda: qi_halves(2)]}
            steps_between(S_QI, INDEX_SLOTS, index_steps)
            group(0, merged({0: [lambda: relu(1)], 3: [lambda: qi_halves(3)], 4: [lambda: relu(2)],
                             8: [lambda: relu(3)]}, kv_q01_steps(0)))
            with act.Fori(1, KV) as g:
                group(g, merged(head_steps(g - 1, 7, 11), kv_q01_steps(g), {11: [lambda: out_high(g - 1)]}))
            last_head_steps = merged(head_steps(KV - 1, 6, 6), {6: [lambda: out_high(KV - 1)]})

            low_banks, high_banks = (0, 4), (4, 8)

            def res_steps(rb, n_done, last=False):
                def halves():
                    act.wait_ge(res_added, rb)
                    take_cross((low_banks, high_banks)[rb % 2], cross[:, :, :], n_done, res_cross)
                if last:
                    return {3: [halves]}
                return {3: [halves], 4: [lambda: res_square(rb)], 5: [lambda: res_high(rb)]}

            def project(first, q, tiles, before):
                slots = tiles // 2
                for j in range(4):
                    steps_between(first, slots, before, at=slots * j)
                    before = res_steps(4 * q + j, first + slots * (j + 1), last=q == 4)
                return before

            def hidden_tiles(fb):
                return hs[:, bass.ds(4 * fb, 4), 0:TOK]

            def gate_steps(fb, done, n_done):
                def halves():
                    if done or not isinstance(fb, int) or fb:
                        act.wait_ge(up_summed, fb + done)
                    take_cross(low_banks, cross[:, :, :], n_done, gate_cross)

                def silu():
                    act.wait_ge(gate_scaled, fb + done + 1)
                    nc.scalar.activation(gated[:, :, :], gated[:, :, :], ACT.Silu).then_inc(gate_silu, 1)
                return {11: [halves], 12: [silu]}

            def up_steps(fb, done, n_done):
                def halves():
                    act.wait_ge(gate_summed, fb + done + 1)
                    take_cross(high_banks, cross[:, :, :], n_done, up_cross)

                def high():
                    act.wait_ge(hidden_done, fb + done + 1)
                    nc.scalar.activation(hidden_tiles(fb), total[:, :, :], ACT.Copy).then_inc(hidden_hi, 1)
                return {3: [halves], 4: [high]}

            def ffn(layer, first, q, before):
                done = FT // 4 * layer
                steps_between(first, 16, before | {10: [lambda: stat(q)]} | gate_steps(0, done, first + 8))
                with act.Fori(1, FT // 4) as i:
                    steps = up_steps(i - 1, done, first + 16 * i) | gate_steps(i, done, first + 16 * i + 8)
                    steps_between(first, 16, steps, 16, i)
                return up_steps(FT // 4 - 1, done, first + 16 * (FT // 4))

            def conv_steps(i, u, n_done):
                def halves():
                    if isinstance(i, int) and i == 0 and u == 0:
                        act.wait_ge(res_added, 12)
                    else:
                        act.wait_ge(cv_summed, 3 * i + u)
                    take_cross((2 * u, 2 * u + 2), cross[:, 0:2, :], n_done, cv_cross)

                def high():
                    act.wait_ge(y_done, i + 1)
                    nc.scalar.activation(hs[:, bass.ds(2 * i, 2), 0:TOK], total[:, 0:2, :], ACT.Copy).then_inc(y_hi, 1)
                return {(7, 11, 3)[u]: [halves]} | ({4: [high]} if u == 2 else {})

            def conv(before):
                steps_between(S_CV, 12, before | conv_steps(0, 0, S_CV + 4) | {10: [lambda: stat(2)]}
                              | conv_steps(0, 1, S_CV + 8))
                with act.Fori(1, 8) as i:
                    n = S_CV + 12 * i
                    steps_between(S_CV, 12, conv_steps(i - 1, 2, n) | conv_steps(i, 0, n + 4)
                                  | conv_steps(i, 1, n + 8), 12, i)
                return conv_steps(7, 2, S_CO)

            before = project(S_AO, 1, KT, last_head_steps)
            before = ffn(0, S_GU0, 1, before)
            before = project(S_DN0, 2, FT, before)
            before = conv(before)
            before = project(S_CO, 3, KT, before)
            before = ffn(1, S_GU1, 3, before)
            before = project(S_DN1, 4, FT, before)
            for step in before[3]:
                step()
            for j in range(4):
                act.wait_ge(row_made, 5 + j)
                nc.scalar.activation(rows[:, 1, WIDE * j:WIDE * (j + 1)], ps[:, 4 + j, :], ACT.Copy).then_inc(row_ready_act, 1)

        @block.vector
        def _(dve):
            tt = nc.vector.tensor_tensor

            def split(first, slots, per_loop=0, i=0, at=0):
                for j in range(at, at + slots):
                    n = first + per_loop * i + j
                    dve.wait_ge(hi_done, n + 1)
                    p = j % RING
                    tt(w_lo[:, p, :], stage[:, p, :], f32(w_hi[:, p, :]), ALU.subtract).then_inc(lo_done, 1)

            def steps_between(first, slots, steps, per_loop=0, i=0, at=0):
                for j in range(slots):
                    split(first, 1, per_loop, i, at + j)
                    for step in steps.get(j, ()):
                        step()

            def stat_sum_step(no):
                dve.wait_ge(sums_done, 4 * no + 4)
                nc.vector.tensor_reduce(colsum[:, :], sums[:, :, :].rearrange("p m t -> p t m"), AX_X,
                                        ALU.add).then_inc(stat_sum, 1)

            def rstd_step(no):
                dve.wait_ge(stat_root, no + 1)
                nc.vector.reciprocal(rstd[:, :], rms[:, :]).then_inc(rstd_ready, 1)

            def res_gain(rb):
                dve.wait_ge(res_added, rb + 1)
                q, j = divmod(rb, 4)
                tt(gated[:, :, :], res[:, 4 * j:4 * j + 4, :], per_tile(gain[:, q, 4 * j:4 * j + 4], TOK),
                   ALU.mult).then_inc(res_gained, 1)

            def res_low(rb):
                dve.wait_ge(res_hi, rb + 1)
                j4 = 4 * (rb % 4)
                tt(xs[:, j4:j4 + 4, TOK:], gated[:, :, :], f32(xs[:, j4:j4 + 4, 0:TOK]),
                   ALU.subtract).then_inc(xs_ready, 1)

            def res_sums(rb):
                dve.wait_ge(res_squared, rb + 1)
                if rb % 4:
                    dve.wait_ge(sums_done, rb)
                    tt(sums[:, :, :], sums[:, :, :], square[:, :, :], ALU.add).then_inc(sums_done, 1)
                else:
                    nc.vector.tensor_copy(sums[:, :, :], square[:, :, :]).then_inc(sums_done, 1)

            def res_steps(rb):
                q, j = divmod(rb, 4)
                bank = 4 * (rb % 2)

                def add():
                    dve.wait_ge(res_cross, rb - 3)
                    tt(total[:, :, :], ps[:, bank:bank + 4, 0:TOK], cross[:, :, :], ALU.add).then_inc(res_summed, 1)
                    dve.wait_ge(res_summed, rb - 3)
                    now = res[:, 4 * j:4 * j + 4, :]
                    tt(now, now, total[:, :, :], ALU.add).then_inc(res_added, 1)
                if q == 4:
                    return {3: [add]}
                steps = {3: [add], 4: [lambda: res_gain(rb)], 5: [lambda: res_low(rb)],
                         6: [lambda: res_sums(rb)]}
                if j == 3:
                    steps[6].append(lambda: stat_sum_step(q))
                return steps

            def project(first, q, tiles, before):
                slots = tiles // 2
                for j in range(4):
                    steps_between(first, slots, before, at=slots * j)
                    before = res_steps(4 * q + j)
                return before

            dve.wait_ge(in_gain, 16)
            for j in range(4):
                if j:
                    dve.wait_ge(xs_ready, j)
                res_gain(j)
                res_low(j)
                for s in ((), (0,), (1,), (2, 3))[j]:
                    dve.wait_ge(hi_done, s + 1)
                    tt(w_lo[:, s, 0:320], stage[:, s, 0:320], f32(w_hi[:, s, 0:320]), ALU.subtract).then_inc(lo_done, 1)
            stat_sum_step(0)
            dve.wait_ge(in_small, 80)

            COS_H, SIN_H, COS_I, SIN_I = (tab[:, i, :] for i in range(4))

            def ki_sum():
                dve.wait_ge(ki_cross, 1)
                tt(kiwi[0:80, :], ps[0:80, 2, 0:TOK], cross[0:80, 0, :], ALU.add).then_inc(qi_summed, 1)

            def ki_scale():
                dve.wait_ge(qi_summed, 1)
                dve.wait_ge(rstd_ready, 1)
                tt(kiwi[0:80, :], kiwi[0:80, :], rstd[0:80, :], ALU.mult).then_inc(ki_scaled, 1)

            def ki_rope():
                dve.wait_ge(ki_turned, 1)
                tt(kir[:, :], ps[:, 6, 0:TOK], COS_I, ALU.mult).then_inc(ki_cos, 1)
                tt(k_sq[:, :], ps[:, 6, TOK:], SIN_I, ALU.mult).then_inc(ki_sin, 1)
                dve.wait_ge(ki_cos, 1)
                dve.wait_ge(ki_sin, 1)
                tt(kir[:, :], kir[:, :], k_sq[:, :], ALU.add).then_inc(ki_ready, 1)
                nc.vector.memset(score[:, :], 0.0).then_inc(score_step, 1)

            def qi_sum(i):
                two = total[:, 0:2, :]
                b0, b1 = QI_BANKS[i % 2]
                dve.wait_ge(qi_cross, i + 1)
                if i:
                    dve.wait_ge(qi_turned, i)
                tt(two, ps[:, b0:b1, 0:TOK], cross[:, 0:2, :], ALU.add).then_inc(qi_summed, 1)
                dve.wait_ge(qi_summed, i + 2)
                tt(two, two, bcast(rstd[:, :], 2), ALU.mult).then_inc(qi_scaled, 1)
                dve.wait_ge(qi_scaled, i + 1)
                tt(gated[:, 0:2, :], two, bcast(COS_I, 2), ALU.mult).then_inc(qi_cos, 1)

            def qi_rope(i):
                dve.wait_ge(qi_turned, i + 1)
                tt(square[:, 0:2, :], ps[:, 7, :].rearrange("p (m t) -> p m t", m=2), bcast(SIN_I, 2),
                   ALU.mult).then_inc(qi_sin, 1)
                dve.wait_ge(qi_cos, i + 1)
                dve.wait_ge(qi_sin, i + 1)
                if i:
                    dve.wait_ge(score_made, i)
                tt(qir[:, :, :], gated[:, 0:2, :], square[:, 0:2, :], ALU.add).then_inc(qi_ready, 1)

            def add_scores(i):
                dve.wait_ge(wt_ready, 1)
                dve.wait_ge(rel_done, i + 1)
                for h in range(4):
                    for a, (c0, c1) in enumerate(COLS):
                        dve.wait_ge(score_step, 8 * i + max(1, 2 * h + a))
                        nc.vector.scalar_tensor_tensor(score[:, c0:c1], index_scores[:, h, c0:c1],
                                                       wt[:, a, 4 * i + h:4 * i + h + 1], score[:, c0:c1],
                                                       ALU.mult, ALU.add).then_inc(score_step, 1)

            def top(count):
                dve.wait_ge(top_step, count)

            def bound_scores():
                dve.wait_ge(score_step, 33)
                tt(score[:, :], score[:, :], bound[:, 0, :], ALU.min).then_inc(top_step, 1)

            def top_rounds(rounds):
                for r in rounds:
                    for a, (c0, c1) in enumerate(COLS):
                        top(max(1, 4 * r + a))
                        nc.vector.max(top8[:, r, a, :], score[:, c0:c1]).then_inc(top_step, 1)
                    for a, (c0, c1) in enumerate(COLS):
                        top(4 * r + 2 + a)
                        nc.vector.match_replace(score[:, c0:c1], top8[:, r, a, :], score[:, c0:c1],
                                                TAKEN).then_inc(top_step, 1)

            def make_mask():
                top(TOPK // 2 + 1)
                nc.vector.tensor_scalar(mask[:, :], score[:, :], TAKEN, -DROP, ALU.is_equal,
                                        ALU.mult).then_inc(top_step, 1)
                top(TOPK // 2 + 2)
                nc.vector.tensor_scalar(mask[:, :], mask[:, :], DROP, None, ALU.add).then_inc(top_step, 1)
                top(TOPK // 2 + 3)
                tt(mask[:, :], mask[:, :], bound[:, 1, :], ALU.min).then_inc(mask_ready, 1)

            def qkv_sum(g, u):
                b0, b1 = STREAM_BANKS[u]
                two = raw[:, 2 * u:2 * u + 2, :]
                dve.wait_ge(qkv_cross, 3 * g + u + 1)
                if not isinstance(g, int) or g:
                    if u == 0:
                        dve.wait_ge(v_made, g)
                        dve.wait_ge(k_gained, g)
                    else:
                        dve.wait_ge(q_gained, 2 * g + u - 2)
                tt(two, ps[:, b0:b1, 0:TOK], cross[:, 0:2, :], ALU.add).then_inc(qkv_summed, 1)
                dve.wait_ge(qkv_summed, 3 * g + u + 1)
                tt(two, two, bcast(rstd[:, :], 2), ALU.mult).then_inc(qkv_scaled, 1)

            def rope_k(p):
                dve.wait_ge(k_gained, p + 1)
                tt(kr[:, :], k_gn[:, :], COS_H, ALU.mult).then_inc(k_cos, 1)
                dve.wait_ge(k_root, p + 1)
                nc.vector.reciprocal(k_rt[:, :], k_rt[:, :]).then_inc(k_inv, 1)
                tt(k_sq[:, :], ps[:, 4, TOK:], SIN_H, ALU.mult).then_inc(k_sin, 1)
                dve.wait_ge(k_cos, p + 1)
                dve.wait_ge(k_sin, p + 1)
                tt(kr[:, :], kr[:, :], k_sq[:, :], ALU.add).then_inc(k_roped, 1)
                dve.wait_ge(k_roped, p + 1)
                dve.wait_ge(k_inv, p + 1)
                tt(kr[:, :], kr[:, :], k_rt[:, :], ALU.mult).then_inc(k_ready, 1)

            def sin_q(p, u):
                dve.wait_ge(q_turned, 2 * p + u + 1)
                tt(sums[:, 2 * u:2 * u + 2, :], ps[:, 6 + u, :].rearrange("p (m t) -> p m t", m=2),
                   bcast(SIN_H, 2), ALU.mult).then_inc(q_sin, 1)

            def cos_q(p):
                dve.wait_ge(q_gained, 2 * p + 2)
                tt(qr[:, :, :], gated[:, :, :], bcast(COS_H, 4), ALU.mult).then_inc(q_cos, 1)

            def rope_q(p):
                dve.wait_ge(q_cos, p + 1)
                dve.wait_ge(q_sin, 2 * p + 2)
                tt(qr[:, :, :], qr[:, :, :], sums[:, :, :], ALU.add).then_inc(q_ready, 1)

            def logit(p):
                dve.wait_ge(q_root, p + 1)
                nc.vector.reciprocal(q_rt[:, :, :], q_rt[:, :, :]).then_inc(q_inv, 1)
                dve.wait_ge(q_inv, p + 1)
                dve.wait_ge(s_made, p + 1)
                dve.wait_ge(mask_ready, 1)
                for h in range(REP):
                    for a, (c0, c1) in enumerate(COLS):
                        nc.vector.scalar_tensor_tensor(prob[:, chunk(a, h)], ps_heads[:, chunk(a, h)],
                                                       q_rt[:, a, h:h + 1], mask[:, c0:c1],
                                                       ALU.mult, ALU.add).then_inc(logit_ready, 1)
                dve.wait_ge(logit_ready, 8 * p + 8)
                for a in range(2):
                    nc.vector.tensor_reduce(peak[:, a, :], heads(prob, a), AX_X, ALU.max).then_inc(peak_done, 1)
                dve.wait_ge(peak_done, 2 * p + 2)
                nc.vector.tensor_scalar(npeak[:, :, :], peak[:, :, :], -1.0, None, ALU.mult).then_inc(npeak_done, 1)

            def normalise(p):
                dve.wait_ge(exp_done, 8 * p + 8)
                nc.vector.reciprocal(rden[:, :, :], den[:, :, :]).then_inc(rden_done, 1)
                dve.wait_ge(rden_done, p + 1)
                for a, (c0, c1) in enumerate(COLS):
                    tt(heads(prob, a), heads(prob, a), per_tile(rden[:, a, :], c1 - c0), ALU.mult).then_inc(prob_ready, 1)

            def out_low(p):
                dve.wait_ge(o_hi, p + 1)
                tiles = bass.ds(4 * p, 4)
                tt(by_query_tile(hs[:, tiles, TOK:]), ps[:, 4:6, :].rearrange("p a (h q) -> p a h q", h=4),
                   by_query_tile(f32(hs[:, tiles, 0:TOK])), ALU.subtract).then_inc(o_read, 1)

            def kv_q01_steps(g):
                return {7: [lambda: qkv_sum(g, 0)], 11: [lambda: qkv_sum(g, 1)]}

            def head_steps(p, at_norm, at_out):
                return merged({2: [lambda: qkv_sum(p, 2)], 3: [lambda: rope_k(p), lambda: sin_q(p, 0)],
                               4: [lambda: cos_q(p)], 5: [lambda: sin_q(p, 1), lambda: rope_q(p)],
                               6: [lambda: logit(p)]},
                              {at_norm: [lambda: normalise(p)]}, {at_out: [lambda: out_low(p)]})

            index_steps = {3: [ki_sum], 4: [lambda: rstd_step(0), ki_scale], 7: [ki_rope, lambda: qi_sum(0)],
                           10: [lambda: qi_rope(0)], 11: [lambda: qi_sum(1)], 12: [lambda: add_scores(0)],
                           14: [lambda: qi_rope(1)], 15: [lambda: qi_sum(2)]}
            steps_between(S_QI, INDEX_SLOTS, index_steps)
            steps_between(S_QKV, 12, merged(
                {0: [lambda: add_scores(1)], 2: [lambda: qi_rope(2)], 3: [lambda: qi_sum(3)],
                 4: [lambda: add_scores(2)], 6: [lambda: qi_rope(3)],
                 8: [lambda: add_scores(3), bound_scores, lambda: top_rounds((0, 1))],
                 9: [lambda: top_rounds((2, 3))], 10: [lambda: top_rounds((4, 5))]},
                kv_q01_steps(0), {11: [lambda: top_rounds((6, 7)), make_mask]}))
            with dve.Fori(1, KV) as g:
                steps_between(S_QKV, 12, merged(kv_q01_steps(g), head_steps(g - 1, 9, 11)), 12, g)
            last_head_steps = head_steps(KV - 1, 6, 6)

            def gate_sum(fb, done):
                dve.wait_ge(gate_cross, fb + done + 1)
                tt(gated[:, :, :], ps[:, 0:4, 0:TOK], cross[:, :, :], ALU.add).then_inc(gate_summed, 1)

            def gate_scale(fb, done):
                dve.wait_ge(gate_summed, fb + done + 1)
                tt(gated[:, :, :], gated[:, :, :], bcast(rstd[:, :], 4), ALU.mult).then_inc(gate_scaled, 1)

            def up_sum(fb, done):
                dve.wait_ge(up_cross, fb + done + 1)
                tt(total[:, :, :], ps[:, 4:8, 0:TOK], cross[:, :, :], ALU.add).then_inc(up_summed, 1)
                dve.wait_ge(up_summed, fb + done + 1)
                tt(total[:, :, :], total[:, :, :], bcast(rstd[:, :], 4), ALU.mult).then_inc(up_scaled, 1)
                dve.wait_ge(up_scaled, fb + done + 1)
                dve.wait_ge(gate_silu, fb + done + 1)
                tt(total[:, :, :], total[:, :, :], gated[:, :, :], ALU.mult).then_inc(hidden_done, 1)

            def hidden_low(fb, done):
                dve.wait_ge(hidden_hi, fb + done + 1)
                tiles = bass.ds(4 * fb, 4)
                tt(hs[:, tiles, TOK:], total[:, :, :], f32(hs[:, tiles, 0:TOK]), ALU.subtract).then_inc(hidden_ready, 1)

            def gate_steps(fb, done):
                return {11: [lambda: gate_sum(fb, done), lambda: gate_scale(fb, done)]}

            def up_steps(fb, done):
                return {3: [lambda: up_sum(fb, done)], 5: [lambda: hidden_low(fb, done)]}

            def ffn(layer, first, q, before):
                done = FT // 4 * layer
                steps_between(first, 16, before | {10: [lambda: rstd_step(q)]} | gate_steps(0, done))
                with dve.Fori(1, FT // 4) as i:
                    steps_between(first, 16, up_steps(i - 1, done) | gate_steps(i, done), 16, i)
                return up_steps(FT // 4 - 1, done)

            def conv_sum(i, u):
                dst = gated if u == 0 else total
                dve.wait_ge(cv_cross, 3 * i + u + 1)
                tt(dst[:, 0:2, :], ps[:, 2 * u:2 * u + 2, 0:TOK], cross[:, 0:2, :], ALU.add).then_inc(cv_summed, 1)

            def conv_scale(i, u):
                dst = gated if u == 0 else total
                dve.wait_ge(cv_summed, 3 * i + u + 1)
                tt(dst[:, 0:2, :], dst[:, 0:2, :], bcast(rstd[:, :], 2), ALU.mult).then_inc(cv_scaled, 1)

            def conv_z(i):
                dve.wait_ge(cv_scaled, 3 * i + 2)
                if isinstance(i, int):
                    dve.wait_ge(zeros_set, 1)
                tt(z[:, :, 2:TOK + 2], gated[:, 0:2, :], total[:, 0:2, :], ALU.mult).then_inc(z_ready, 1)

            def conv_taps(i, which):
                dve.wait_ge(z_ready, i + 1)
                for t in which:
                    for m in range(2):
                        tap = taps[:, t, bass.ds(2 * i + m, 1)]
                        src = z[:, m, t:t + TOK]
                        if t == 0:
                            ins = nc.vector.tensor_scalar(ytap[:, m, :], src, tap, None, ALU.mult)
                        else:
                            dve.wait_ge(tap_step, 6 * i + 2 * t + m - 1)
                            ins = nc.vector.scalar_tensor_tensor(ytap[:, m, :], src, tap, ytap[:, m, :],
                                                                 ALU.mult, ALU.add)
                        ins.then_inc(tap_step, 1)

            def conv_gate(i):
                dve.wait_ge(cv_scaled, 3 * i + 3)
                dve.wait_ge(tap_step, 6 * i + 6)
                tt(total[:, 0:2, :], total[:, 0:2, :], ytap[:, :, :], ALU.mult).then_inc(y_done, 1)

            def conv_low(i):
                dve.wait_ge(y_hi, i + 1)
                tiles = bass.ds(2 * i, 2)
                tt(hs[:, tiles, TOK:], total[:, 0:2, :], f32(hs[:, tiles, 0:TOK]), ALU.subtract).then_inc(y_ready, 1)

            def c_steps(i):
                return {7: [lambda: conv_sum(i, 0), lambda: conv_scale(i, 0)]}

            def u_steps(i):
                return {11: [lambda: conv_sum(i, 1), lambda: conv_scale(i, 1), lambda: conv_z(i)]}

            def b_steps(i):
                return {0: [lambda: conv_taps(i, (0, 1))], 1: [lambda: conv_taps(i, (2,))],
                        3: [lambda: conv_sum(i, 2), lambda: conv_scale(i, 2), lambda: conv_gate(i)],
                        5: [lambda: conv_low(i)]}

            def conv(before):
                steps_between(S_CV, 12, before | {7: [lambda: conv_sum(0, 0)],
                                                  10: [lambda: rstd_step(2), lambda: conv_after_stat()]} | u_steps(0))
                with dve.Fori(1, 8) as i:
                    steps_between(S_CV, 12, b_steps(i - 1) | c_steps(i) | u_steps(i), 12, i)
                return b_steps(7)

            def conv_after_stat():
                dve.wait_ge(rstd_ready, 3)
                conv_scale(0, 0)
                nc.vector.memset(z[:, :, 0:2], 0.0).then_inc(zeros_set, 1)

            before = project(S_AO, 1, KT, last_head_steps)
            before = ffn(0, S_GU0, 1, before)
            before = project(S_DN0, 2, FT, before)
            before = conv(before)
            before = project(S_CO, 3, KT, before)
            before = ffn(1, S_GU1, 3, before)
            before = project(S_DN1, 4, FT, before)
            for step in before[3]:
                step()
            for j in range(4):
                dve.wait_ge(row_made, j + 1)
                nc.vector.tensor_copy(rows[:, 0, WIDE * j:WIDE * (j + 1)], ps[:, j, :]).then_inc(row_ready, 1)

        @block.gpsimd
        def _(pool):
            pool.memset(eps[:, 0:1], EPS).then_inc(const_set, 1)
            pool.memset(eps[:, 1:2], EPS * HD).then_inc(const_set, 1)
            for j in range(4):
                pool.wait_ge(res_squared, j + 1)
                if j:
                    pool.wait_ge(sums_done, j)
                    nc.gpsimd.tensor_tensor(sums[:, :, :], sums[:, :, :], square[:, :, :], ALU.add).then_inc(sums_done, 1)
                else:
                    nc.gpsimd.tensor_copy(sums[:, :, :], square[:, :, :]).then_inc(sums_done, 1)


def shape_constants():
    tables = np.zeros((P, 4, TOK), np.float32)
    pos = np.arange(TOK, dtype=np.float32)
    for at, dim in ((0, HD), (2, ID)):
        inv = np.float32(1.0) / np.float32(10000.0) ** (np.arange(0, dim, 2, dtype=np.float32) / np.float32(dim))
        angle = (pos[None, :] * inv[:, None]).astype(np.float32).astype(np.float64)
        rows = np.arange(P) % (dim // 2)
        tables[:, at] = np.cos(angle)[rows]
        tables[:, at + 1] = np.sin(angle)[rows]

    def rotation(dim):
        r = np.zeros((P, P), np.float32)
        for m in range(P):
            first = m % dim < dim // 2
            r[m + dim // 2 if first else m - dim // 2, m] = -1.0 if first else 1.0
        return r

    dup = np.zeros((P, P), np.float32)
    for m in range(P):
        dup[m % ID, m] = 1.0
    dup_rot = np.zeros((P, P), np.float32)
    rot = rotation(ID)
    for m in range(P):
        dup_rot[:ID, m] = rot[:ID, m % ID]
    mats = np.stack([np.eye(P, dtype=np.float32), np.full((P, P), 1.0 / D, np.float32),
                     np.full((P, P), 1.0 / HD, np.float32), rotation(HD), rotation(ID), dup, dup_rot], axis=1)
    bounds = np.zeros((P, 2, 384), np.float32)
    for a, (c0, c1) in enumerate(COLS):
        query = a * P + np.arange(P)[:, None]
        key = np.arange(c1 - c0)[None, :]
        bounds[:, 0, c0:c1] = np.where(key <= query, np.float32(-FILL), np.float32(FILL))
        bounds[:, 1, c0:c1] = np.where(key <= query, np.float32(0.0), np.float32(DROP))
    return tables, np.ascontiguousarray(mats), bounds


def kernel(x, attn_norm, attn_w_in, attn_q_norm, attn_k_norm, attn_w_out, conv_norm, conv_w_in, conv_w,
           conv_w_out, ffn_norm, ffn_w_gate, ffn_w_up, ffn_w_down):
    import concourse.bacc as bacc
    from concourse.bass_utils import run_bass_kernel_spmd

    def by_partition(a):
        a = np.asarray(a).reshape(-1, KT, P)
        return np.ascontiguousarray(a.transpose(2, 0, 1))

    x, attn_norm, conv_norm, ffn_norm = (np.asarray(a) for a in (x, attn_norm, conv_norm, ffn_norm))
    tables, mats, bounds = shape_constants()
    arrays = {
        "x": x[0],
        "attn_w_in": attn_w_in[0], "attn_w_out": attn_w_out[0],
        "conv_w_in": conv_w_in[0], "conv_w_out": conv_w_out[0],
        "w_gate": ffn_w_gate, "w_up": ffn_w_up, "w_down": ffn_w_down,
        "gains": by_partition(np.stack([attn_norm[0], ffn_norm[0], conv_norm[0], ffn_norm[1]])),
        "head_gains": np.stack([np.asarray(attn_q_norm)[0], np.asarray(attn_k_norm)[0]], axis=1),
        "conv_taps": by_partition(np.asarray(conv_w)[0]),
        "tables": tables, "mats": mats, "bounds": bounds,
    }
    arrays = {f"in_{k}": np.ascontiguousarray(v) for k, v in arrays.items()}
    nc = bacc.Bacc("TRN2", target_bir_lowering=False, num_devices=1)
    args = [nc.dram_tensor(k, v.shape, mybir.dt.from_np(v.dtype), kind="ExternalInput").ap() for k, v in arrays.items()]
    out = nc.dram_tensor("out", (TOK, D), F32, kind="ExternalOutput").ap()
    trunk(nc, *args, out)
    r = run_bass_kernel_spmd(nc, [arrays], core_ids=[0])
    return np.asarray(r.results[0]["out"]).reshape(1, TOK, D)
```

```python
from contextlib import ExitStack

import numpy as np

import concourse.bass as bass
from concourse import mybir
from concourse.alu_op_type import AluOpType as ALU

ACT = mybir.ActivationFunctionType
F32 = mybir.dt.float32
F32R = mybir.dt.float32r
AX_X = mybir.AxisListType.X

P = 128
TOK = 256
D = 2048
KT = D // P
HEADS, KV, REP, HD = 16, 4, 4, 128
IH, ID = 16, 64
F = 5632
FT = F // P
TOPK = 64
EPS = 1e-6
RING = 4
SLOT = 1024
WIDE, NARROW = 512, 256
COLS = ((0, 128), (128, 384))
FILL = -3.0e38
TAKEN = -3.3e38
DROP = -1.0e30

S_KI = 0
S_QI = S_KI + 4
S_QKV = S_QI + 4 * 4
S_AO = S_QKV + KV * 12
S_GU0 = S_AO + 4 * 8
S_DN0 = S_GU0 + (FT // 4) * 16
S_CV = S_DN0 + 4 * 22
S_CO = S_CV + 8 * 12
S_GU1 = S_CO + 4 * 8
S_DN1 = S_GU1 + (FT // 4) * 16
S_END = S_DN1 + 4 * 22


def trunk(nc, x, attn_w_in, attn_w_out, conv_w_in, conv_w_out, w_gate, w_up, w_down,
          gains, head_gains, conv_taps, tables, mats, bounds, out):
    with ExitStack() as ctx:
        def sb(name, shape, dt=F32, stack=ctx):
            return stack.enter_context(nc.sbuf_tensor(name, shape, dt))

        def sem(name):
            return ctx.enter_context(nc.semaphore(name))

        stage = sb("stage", [P, RING, SLOT])
        w_hi = sb("w_hi", [P, RING, SLOT], F32R)
        w_lo = sb("w_lo", [P, RING, SLOT], F32R)
        xs = sb("xs", [P, KT, 2 * TOK], F32R)
        res = sb("res", [P, KT, TOK])
        gain = sb("gain", [P, 4, KT])
        hgain = sb("hgain", [P, 2])
        taps = sb("taps", [P, 3, KT])
        mat = sb("mat", [P, 2, P])
        cross = sb("cross", [P, 4, TOK])
        total = sb("total", [P, 4, TOK])
        gated = sb("gated", [P, 4, TOK])
        square = sb("square", [P, 4, TOK])
        sums = sb("sums", [P, 4, TOK])
        colsum = sb("colsum", [P, TOK])
        rstd = sb("rstd", [P, TOK])
        eps = sb("eps", [P, 2])

        part = ExitStack()
        sb("head_outputs", [P, KT, 2 * TOK], F32R, stack=part)
        tab = sb("tab", [P, 4, TOK], stack=part)
        mat_a = sb("mat_a", [P, 5, P], stack=part)
        bound = sb("bound", [P, 2, 384], stack=part)
        kiwi = sb("kiwi", [P, TOK], stack=part)
        kir = sb("kir", [P, TOK], stack=part)
        qir = sb("qir", [P, 2, TOK], stack=part)
        wt = sb("wt", [P, 2, IH], stack=part)
        score = sb("score", [P, 384], stack=part)
        top8 = sb("top8", [P, 8, 2, 8], stack=part)
        mask = sb("mask", [P, 384], stack=part)
        raw = sb("raw", [P, 6, TOK], stack=part)
        k_sq = sb("k_sq", [P, TOK], stack=part)
        k_gn = sb("k_gn", [P, TOK], stack=part)
        k_rt = sb("k_rt", [P, TOK], stack=part)
        kr = sb("kr", [P, TOK], stack=part)
        qr = sb("qr", [P, 4, TOK], stack=part)
        vt = sb("vt", [P, 2, HD], stack=part)
        q_rt = sb("q_rt", [P, 2, 4], stack=part)
        peak = sb("peak", [P, 2, 4], stack=part)
        npeak = sb("npeak", [P, 2, 4], stack=part)
        den = sb("den", [P, 2, 4], stack=part)
        rden = sb("rden", [P, 2, 4], stack=part)
        early = ExitStack()
        xin = sb("xin", [P, 2, D], stack=early)
        early.close()
        late = ExitStack()
        prob = sb("prob", [P, 1536], stack=late)
        pt = sb("pt", [P, 1536], stack=late)
        late.close()
        part.close()
        whole = ExitStack()
        hs = sb("hs", [P, FT, 2 * TOK], F32R, stack=whole)
        whole.close()
        rows = [buf[:, :, :].rearrange("p (a b) t -> p a (b t)", a=2) for buf in (square, sums, gated, cross)]

        rms = colsum
        ytap = square[:, 0:2, :]
        z = sums[:, :, :].rearrange("p m t -> p (m t)")[:, 0:2 * (TOK + 2)].rearrange("p (m t) -> p m t", m=2)

        def f32(ap):
            return ap.bitcast(F32)

        ps = ctx.enter_context(nc.psum_tensor("ps", [P, 8, 512], F32))
        COS_H, SIN_H, COS_I, SIN_I = (tab[:, i, :] for i in range(4))
        ps_heads = ps[:, 4:7, :].rearrange("p b c -> p (b c)")

        IDENT, MEAN_D = (mat[:, i, :] for i in range(2))
        MEAN_H, ROT_H, ROT_I, DUP, DUP_ROT = (mat_a[:, i, :] for i in range(5))

        in_ident = sem("in_ident")
        in_x = [sem(f"in_x{j}") for j in range(4)]
        in_gain = sem("in_gain")
        in_small = sem("in_small")
        loaded = [sem(f"loaded{i}") for i in range(RING)]
        v_loaded = [sem(f"v_loaded{i}") for i in range(RING)]
        hi_done = sem("hi_done")
        lo_done = sem("lo_done")
        slot_used = sem("slot_used")
        const_set = sem("const_set")
        x_turned = sem("x_turned")
        res_cross = sem("res_cross")
        res_summed = sem("res_summed")
        res_added = sem("res_added")
        res_squared = sem("res_squared")
        res_gained = sem("res_gained")
        res_hi = sem("res_hi")
        xs_ready = sem("xs_ready")
        sums_done = sem("sums_done")
        stat_sum = sem("stat_sum")
        stat_made = sem("stat_made")
        stat_root = sem("stat_root")
        rstd_ready = sem("rstd_ready")
        ki_scaled = sem("ki_scaled")
        ki_turned = sem("ki_turned")
        ki_cross = sem("ki_cross")
        ki_cos = sem("ki_cos")
        ki_sin = sem("ki_sin")
        ki_ready = sem("ki_ready")
        wt_ready = sem("wt_ready")
        qi_cross = sem("qi_cross")
        qi_summed = sem("qi_summed")
        qi_scaled = sem("qi_scaled")
        qi_turned = sem("qi_turned")
        qi_cos = sem("qi_cos")
        qi_sin = sem("qi_sin")
        qi_ready = sem("qi_ready")
        score_made = sem("score_made")
        rel_done = sem("rel_done")
        score_step = sem("score_step")
        top_step = sem("top_step")
        mask_ready = sem("mask_ready")
        qkv_cross = sem("qkv_cross")
        qkv_summed = sem("qkv_summed")
        qkv_scaled = sem("qkv_scaled")
        k_squared = sem("k_squared")
        k_gained = sem("k_gained")
        k_made = sem("k_made")
        k_root = sem("k_root")
        k_inv = sem("k_inv")
        k_cos = sem("k_cos")
        k_sin = sem("k_sin")
        k_roped = sem("k_roped")
        k_ready = sem("k_ready")
        v_made = sem("v_made")
        v_ready = sem("v_ready")
        q_squared = sem("q_squared")
        q_gained = sem("q_gained")
        q_turned = sem("q_turned")
        q_var = sem("q_var")
        q_root = sem("q_root")
        q_inv = sem("q_inv")
        q_cos = sem("q_cos")
        q_sin = sem("q_sin")
        q_ready = sem("q_ready")
        s_made = sem("s_made")
        logit_ready = sem("logit_ready")
        peak_done = sem("peak_done")
        npeak_done = sem("npeak_done")
        exp_done = sem("exp_done")
        rden_done = sem("rden_done")
        prob_ready = sem("prob_ready")
        pt_made = sem("pt_made")
        pt_copied = sem("pt_copied")
        o_made = sem("o_made")
        o_hi = sem("o_hi")
        o_read = sem("o_read")
        gate_cross = sem("gate_cross")
        gate_summed = sem("gate_summed")
        gate_scaled = sem("gate_scaled")
        gate_silu = sem("gate_silu")
        up_cross = sem("up_cross")
        up_summed = sem("up_summed")
        up_scaled = sem("up_scaled")
        hidden_done = sem("hidden_done")
        hidden_hi = sem("hidden_hi")
        hidden_ready = sem("hidden_ready")
        cv_cross = sem("cv_cross")
        cv_summed = sem("cv_summed")
        cv_scaled = sem("cv_scaled")
        zeros_set = sem("zeros_set")
        z_ready = sem("z_ready")
        tap_step = sem("tap_step")
        y_done = sem("y_done")
        y_hi = sem("y_hi")
        y_ready = sem("y_ready")
        row_made = sem("row_made")
        row_ready = sem("row_ready")
        row_ready_dve = sem("row_ready_dve")
        last_cross = sem("last_cross")
        last_summed = sem("last_summed")
        last_added = sem("last_added")
        stored = sem("stored")

        def bcast(ap, tiles):
            return ap.unsqueeze(1).to_broadcast([P, tiles, ap.shape[1]])

        def per_tile(ap, width):
            return ap.unsqueeze(2).to_broadcast([P, ap.shape[1], width])

        index_scores = prob[:, :].rearrange("p (h c) -> p h c", h=4)

        def chunk(a, h):
            return slice(P * h, P * (h + 1)) if a == 0 else slice(512 + TOK * h, 512 + TOK * (h + 1))

        def heads(ap, a):
            return (ap[:, 0:512] if a == 0 else ap[:, 512:1536]).rearrange("p (h c) -> p h c", h=4)

        def merged(*steps):
            out = {}
            for part_steps in steps:
                for at, some in part_steps.items():
                    out[at] = out.get(at, []) + some
            return out

        X_BANKS = (2, 6)
        STREAM_BANKS = ((0, 2), (2, 4), (0, 2))
        QI_BANKS = ((0, 2), (2, 4))
        START_WIDTHS = (4 * (ID + IH), SLOT)
        X_GAINED = (gated, total)
        INDEX_SLOTS = 16

        block = ctx.enter_context(nc.Block())

        @block.sync
        def _(sp):
            def load(n, pos, rows_of, width):
                k = rows_of.shape[0] // P
                if not isinstance(n, int) or n >= RING:
                    sp.wait_ge(lo_done, n - (RING - 1))
                dst = stage[:, pos, 0:k * width].rearrange("p (k n) -> p k n", k=k)
                sp.dma_start(dst, rows_of.rearrange("(k p) n -> p k n", p=P)).then_inc(loaded[pos], 16)

            def load_block(n, w, base, col, width, tiles):
                per = SLOT // width if width >= NARROW else 4
                for s in range(tiles // per):
                    load(n + s, s % RING, w[s * per * P:(s + 1) * per * P, base:][:, bass.ds(col, width)], width)

            def load_x(j):
                sp.dma_start(xin[:, :, WIDE * j:WIDE * (j + 1)],
                             x[:, WIDE * j:WIDE * (j + 1)].rearrange("(a p) n -> p a n", p=P)).then_inc(in_x[j], 16)

            sp.dma_start(mat.ap(), mats[:, 0:2, :]).then_inc(in_ident, 16)
            load_x(0)
            load_x(1)
            w_in = attn_w_in
            for c in range(4):
                rows_of = w_in[c * WIDE:(c + 1) * WIDE, D + 2 * KV * HD:]
                load(S_KI + 2 * c, 2 * c % RING, rows_of[:, IH * ID:IH * ID + ID + IH], ID + IH)
                load(S_KI + 2 * c + 1, (2 * c + 1) % RING, rows_of[:, 0:NARROW], NARROW)
                if c < 2:
                    load_x(c + 2)
            with sp.Fori(1, 4) as i:
                load_block(S_QI + 4 * i, w_in, D + 2 * KV * HD, NARROW * i, NARROW, KT)
            with sp.Fori(0, KV) as g:
                n = S_QKV + 12 * g
                for s in range(4):
                    rows4 = slice(s * 4 * P, (s + 1) * 4 * P)
                    sp.wait_ge(lo_done, n + s - (RING - 1))
                    dst = stage[:, s, :].rearrange("p (k n) -> p k n", k=4)
                    for side, arrived in ((0, loaded[s]), (1, v_loaded[s])):
                        src = w_in[rows4, D + side * KV * HD:][:, bass.ds(HD * g, HD)]
                        sp.dma_start(dst[:, :, side * HD:(side + 1) * HD],
                                     src.rearrange("(k p) n -> p k n", p=P)).then_inc(arrived, 16)
                load_block(n + 4, w_in, 0, WIDE * g, NARROW, KT)
                load_block(n + 8, w_in, NARROW, WIDE * g, NARROW, KT)

            def load_wide(first, w, tiles):
                slots = tiles // 2
                with sp.Fori(0, 2) as i:
                    for u in range(2):
                        for s in range(slots):
                            load(first + 2 * slots * i + u * slots + s, (u * slots + s) % RING,
                                 w[s * 2 * P:(s + 1) * 2 * P, WIDE * u:][:, bass.ds(2 * WIDE * i, WIDE)], WIDE)

            def load_ffn(first, layer):
                with sp.Fori(0, FT // 4) as i:
                    load_block(first + 16 * i, w_gate[layer], 0, WIDE * i, WIDE, KT)
                    load_block(first + 16 * i + 8, w_up[layer], 0, WIDE * i, WIDE, KT)

            load_wide(S_AO, attn_w_out, KT)
            load_ffn(S_GU0, 0)
            load_wide(S_DN0, w_down[0], FT)
            with sp.Fori(0, 8) as i:
                for u, base in enumerate((D, 2 * D, 0)):
                    col = NARROW * i if u < 2 else (P * i) * 2
                    load_block(S_CV + 12 * i + 4 * u, conv_w_in, base, col, NARROW, KT)
            load_wide(S_CO, conv_w_out, KT)
            load_ffn(S_GU1, 1)
            load_wide(S_DN1, w_down[1], FT)

            for j in range(4):
                cols = slice(WIDE * j, WIDE * (j + 1))
                sp.wait_ge(row_ready, j + 1)
                if j < 3:
                    sp.dma_start(out[:, cols].rearrange("(a p) n -> p a n", p=P), rows[j]).then_inc(stored, 16)
                else:
                    sp.dma_start(out[0:P, cols], rows[j][:, 0, :]).then_inc(stored, 16)
                    sp.wait_ge(row_ready_dve, 1)
                    sp.dma_start(out[P:, cols], rows[j][:, 1, :]).then_inc(stored, 16)
            sp.wait_ge(stored, 80)

        @block.tensor
        def _(pe):
            def stream(n, banks, width, tiles, moving, ready=None, count=P, place=0, after=None,
                       only=None, every=1):
                per = SLOT // width if width >= NARROW else 4
                step = width if width >= NARROW else count
                for s in only or range(tiles // per):
                    pe.wait_ge(lo_done, n + every * s + 1)
                    for kk in range(per):
                        k = s * per + kk
                        if ready is not None:
                            ready(k)
                        rhs = moving(k)
                        for m in range((width + P - 1) // P):
                            at = slice(kk * step + m * P, kk * step + m * P + count)
                            bank = ps[0:count, banks[m], :]
                            slot = (place + every * s) % RING
                            full = (bank, w_hi[:, slot, at], rhs)
                            low = (bank[:, TOK:], w_lo[:, slot, at], rhs[:, 0:TOK])
                            last = k == tiles - 1
                            if last:
                                pe.matmul(*low, start=False, stop=False)
                                mm = pe.matmul(*full, start=False, stop=True)
                            else:
                                pe.matmul(*full, start=k == 0, stop=False)
                                mm = pe.matmul(*low, start=False, stop=False)
                    mm.then_inc(slot_used, 1)
                    for other in (after or {}).get(s, ()):
                        other()

            low_banks, high_banks = (0, 1, 2, 3), (4, 5, 6, 7)

            def xs_tile(k):
                return xs[:, k, :]

            def hs_tile(k):
                return hs[:, k, :]

            def xs_wait(stage_no):
                def ready(k):
                    if k % 4 == 0:
                        pe.wait_ge(xs_ready, 4 * stage_no + k // 4 + 1)
                return ready

            def stat(no):
                pe.wait_ge(stat_sum, no + 1)
                pe.matmul(ps[:, 7, 0:TOK], MEAN_D, colsum[:, :], start=True, stop=True).then_inc(stat_made, 1)

            pe.wait_ge(in_ident, 16)

            def turn_x(j):
                pe.wait_ge(in_x[j], 16)
                if j >= 2:
                    pe.wait_ge(res_added, j - 1)
                for m in range(4):
                    for a in range(2):
                        at = TOK * (m % 2) + P * a
                        mm = pe.transpose(ps[:, X_BANKS[j % 2] + m // 2, at:at + P],
                                          xin[:, a, (4 * j + m) * P:(4 * j + m + 1) * P], IDENT)
                mm.then_inc(x_turned, 1)

            def ki_turn():
                pe.wait_ge(ki_scaled, 1)
                pe.wait_ge(in_small, 80)
                pe.matmul(ps[:, 6, 0:TOK], DUP[0:ID, :], kiwi[0:ID, :], start=True, stop=True)
                pe.matmul(ps[:, 6, TOK:], DUP_ROT[0:ID, :], kiwi[0:ID, :], start=True, stop=True)
                for a in range(2):
                    mm = pe.transpose(ps[:, 5, a * P:a * P + 80], kiwi[0:80, a * P:(a + 1) * P], IDENT[0:80, 0:80])
                mm.then_inc(ki_turned, 1)

            def qi_turn(i):
                pe.wait_ge(qi_scaled, i + 1)
                if i:
                    pe.wait_ge(rel_done, i)
                else:
                    pe.wait_ge(stat_root, 1)
                for m in range(2):
                    mm = pe.matmul(ps[:, 7, m * TOK:(m + 1) * TOK], ROT_I, total[:, m, :], start=True, stop=True)
                mm.then_inc(qi_turned, 1)

            def score_heads(i):
                pe.wait_ge(qi_ready, i + 1)
                if i == 0:
                    pe.wait_ge(ki_ready, 1)
                    pe.wait_ge(wt_ready, 1)
                for h in range(4):
                    half = slice(ID * (h % 2), ID * (h % 2) + ID)
                    for a, (c0, c1) in enumerate(COLS):
                        mm = pe.matmul(ps[:, 4 + h, c0:c1], qir[half, h // 2, a * P:(a + 1) * P],
                                       kir[half, 0:c1 - c0], start=True, stop=True)
                mm.then_inc(score_made, 1)

            for j in range(3):
                turn_x(j)
            for c in range(4):
                stream(S_KI, (4,), ID + IH, KT, xs_tile, xs_wait(0), count=ID + IH, only=(c,), every=2)
                stream(S_KI + 1, (0, 1), NARROW, KT, xs_tile, place=1, only=(c,), every=2)
                if c == 0:
                    turn_x(3)
            pe.wait_ge(res_added, 4)
            stream(S_QI + 4, (2, 3), NARROW, KT, xs_tile,
                   after={0: [lambda: stat(0)], 2: [lambda: qi_turn(0)], 3: [ki_turn]})
            pe.wait_ge(qi_summed, 2)
            stream(S_QI + 8, (0, 1), NARROW, KT, xs_tile,
                   after={1: [lambda: score_heads(0)], 2: [lambda: qi_turn(1)]})
            pe.wait_ge(qi_summed, 3)
            stream(S_QI + 12, (2, 3), NARROW, KT, xs_tile,
                   after={0: [lambda: score_heads(1)], 2: [lambda: qi_turn(2)]})

            def turn_kvq(g):
                pe.wait_ge(k_squared, g + 1)
                pe.matmul(ps[:, 4, 0:TOK], MEAN_H, k_sq[:, :], start=True, stop=True)
                pe.wait_ge(k_gained, g + 1)
                pe.matmul(ps[:, 4, TOK:], ROT_H, k_gn[:, :], start=True, stop=True).then_inc(k_made, 1)
                for a in range(2):
                    mm = pe.transpose(ps[:, 5, a * P:(a + 1) * P], raw[:, 1, a * P:(a + 1) * P], IDENT)
                mm.then_inc(v_made, 1)
                pe.wait_ge(q_gained, 2 * g + 1)
                for m in range(2):
                    mm = pe.matmul(ps[:, 6, m * TOK:(m + 1) * TOK], ROT_H, gated[:, m, :], start=True, stop=True)
                mm.then_inc(q_turned, 1)

            def turn_q23(p):
                pe.wait_ge(q_gained, 2 * p + 2)
                for m in range(2):
                    mm = pe.matmul(ps[:, 7, m * TOK:(m + 1) * TOK], ROT_H, gated[:, 2 + m, :], start=True, stop=True)
                mm.then_inc(q_turned, 1)

            def vars_q(p):
                pe.wait_ge(q_squared, 2 * p + 2)
                pe.wait_ge(v_ready, p + 1)
                for a in range(2):
                    for h in range(REP):
                        mm = pe.matmul(ps[:, 5, 4 * a + h:4 * a + h + 1], square[:, h, a * P:(a + 1) * P],
                                       MEAN_H[:, 0:1], start=True, stop=True)
                mm.then_inc(q_var, 1)

            def logits(p):
                pe.wait_ge(k_ready, p + 1)
                pe.wait_ge(q_ready, p + 1)
                pe.wait_ge(q_root, p + 1)
                for a, (c0, c1) in enumerate(COLS):
                    for h in range(REP):
                        mm = pe.matmul(ps_heads[:, chunk(a, h)], qr[:, h, a * P:(a + 1) * P], kr[:, 0:c1 - c0],
                                       start=True, stop=True)
                    mm.then_inc(s_made, 1)

            def turn_prob(p):
                for a, blocks in enumerate((range(4), range(4, 12))):
                    pe.wait_ge(prob_ready, 2 * p + a + 1)
                    for c in blocks:
                        mm = pe.transpose(ps_heads[:, c * P:(c + 1) * P], prob[:, c * P:(c + 1) * P], IDENT)
                    mm.then_inc(pt_made, 1)

            def outputs(p):
                pe.wait_ge(pt_copied, 2 * p + 1)
                pe.matmul(ps[:, 4, :], vt[:, 0, :], pt[:, 0:512], start=True, stop=True).then_inc(o_made, 1)
                pe.wait_ge(pt_copied, 2 * p + 2)
                later = heads(pt, 1)
                pe.matmul(ps[:, 5, :].rearrange("p (h q) -> p h q", h=4), vt[:, 0, :], later[:, :, 0:P],
                          start=True, stop=False)
                pe.matmul(ps[:, 5, :].rearrange("p (h q) -> p h q", h=4), vt[:, 1, :], later[:, :, P:],
                          start=False, stop=True).then_inc(o_made, 1)

            def group(g, p, after_kv, after_q01, after_q23):
                n = S_QKV + 12 * g
                if p is None:
                    pe.wait_ge(qi_summed, 4)
                else:
                    pe.wait_ge(qkv_summed, 3 * g)
                stream(n, (0, 1), NARROW, KT, xs_tile, after=after_kv)
                if p is None:
                    pe.wait_ge(qi_summed, 5)
                stream(n + 4, (2, 3), NARROW, KT, xs_tile, after=after_q01)
                pe.wait_ge(qkv_summed, 3 * g + 1)
                stream(n + 8, (0, 1), NARROW, KT, xs_tile, after=after_q23)
                if p is None:
                    pe.wait_ge(rel_done, 4)
                else:
                    pe.wait_ge(o_read, 2 * g)
                turn_kvq(g)

            group(0, None, {0: [lambda: score_heads(2)], 2: [lambda: qi_turn(3)]},
                  {0: [lambda: score_heads(3)]}, {})
            with pe.Fori(1, KV) as g:
                group(g, g - 1, {1: [lambda: turn_q23(g - 1), lambda: vars_q(g - 1)], 3: [lambda: logits(g - 1)]},
                      {}, {0: [lambda: turn_prob(g - 1)], 1: [lambda: outputs(g - 1)]})

            def ao_ready(k):
                if k in (0, KT - REP):
                    pe.wait_ge(o_read, 2 * KV if k else 2 * (KV - 1))
            last = KV - 1
            for j in range(4):
                if j == 0:
                    pe.wait_ge(qkv_summed, 3 * KV)
                elif j == 1:
                    pe.wait_ge(o_read, 2 * KV)
                else:
                    pe.wait_ge(res_added, 3 + j)
                stream(S_AO + 8 * j, (low_banks, high_banks)[j % 2], WIDE, KT, hs_tile, None if j else ao_ready,
                       after=None if j else {0: [lambda: turn_q23(last), lambda: vars_q(last)],
                                             1: [lambda: logits(last)],
                                             4: [lambda: turn_prob(last), lambda: outputs(last)]})

            def project(first, q, tiles, waits, ready=None):
                slots = tiles // 2
                with pe.Fori(0, 2) as i:
                    for u in range(2):
                        waits(u)
                        pe.wait_ge(res_added, 4 * q + 2 * i + u - 1)
                        stream(first + 2 * slots * i + slots * u, (low_banks, high_banks)[u], WIDE, tiles,
                               hs_tile, ready, place=slots * u % RING)

            def ffn(layer, first, q):
                def body(i, first_time):
                    fb = (FT // 4) * layer + i
                    if first_time:
                        pe.wait_ge(res_summed, 4 * (q - 1) + 3)
                    else:
                        pe.wait_ge(gate_summed, fb)
                    stream(first + 16 * i, low_banks, WIDE, KT, xs_tile, xs_wait(q) if first_time else None,
                           after={6: [lambda: stat(q)]} if first_time else None)
                    if first_time:
                        pe.wait_ge(stat_root, q + 1)
                    else:
                        pe.wait_ge(up_summed, fb)
                    stream(first + 16 * i + 8, high_banks, WIDE, KT, xs_tile)
                body(0, True)
                with pe.Fori(1, FT // 4) as i:
                    body(i, False)

            def down(layer, first, q):
                blocks = (FT // 4) * (layer + 1)

                def waits(u):
                    pe.wait_ge(up_summed if u else gate_summed, blocks)

                def ready(k):
                    if k in (0, FT - 4):
                        pe.wait_ge(hidden_ready, blocks if k else blocks - 1)
                project(first, q, FT, waits, ready)

            ffn(0, S_GU0, 1)
            down(0, S_DN0, 2)

            def conv(i, first_time):
                n = S_CV + 12 * i
                if first_time:
                    pe.wait_ge(res_summed, 7)
                else:
                    pe.wait_ge(cv_summed, 3 * i - 2)
                stream(n, (0, 1), NARROW, KT, xs_tile, xs_wait(2) if first_time else None)
                if not first_time:
                    pe.wait_ge(cv_summed, 3 * i - 1)
                stream(n + 4, (2, 3), NARROW, KT, xs_tile)
                if first_time:
                    stat(2)
                else:
                    pe.wait_ge(cv_summed, 3 * i)
                stream(n + 8, (4, 5), NARROW, KT, xs_tile)
            conv(0, True)
            with pe.Fori(1, 8) as i:
                conv(i, False)

            def co_waits(u):
                pe.wait_ge(cv_summed, 23 + u)

            def y_wait(k):
                if k in (0, KT - 2):
                    pe.wait_ge(y_ready, 8 if k else 7)

            project(S_CO, 3, KT, co_waits, y_wait)
            ffn(1, S_GU1, 3)

            def turn_rows(j, tiles):
                b = 4 * (j % 2) if j < 3 else 0
                for m in tiles:
                    for a in range(2):
                        mm = pe.transpose(ps[:, b + a, m * P:(m + 1) * P], res[:, 4 * j + m, a * P:(a + 1) * P], IDENT)
                return mm

            def turn_block(j):
                pe.wait_ge(res_added, 17 + j)
                turn_rows(j, range(4)).then_inc(row_made, 1)

            def hidden_wait(k):
                if k in (0, FT - 4):
                    pe.wait_ge(hidden_ready, 2 * (FT // 4) if k else 2 * (FT // 4) - 1)
            for j in range(4):
                if j < 2:
                    pe.wait_ge(up_summed if j else gate_summed, 2 * (FT // 4))
                else:
                    pe.wait_ge(row_ready, j - 1)
                    pe.wait_ge(res_added, 15 + j)
                stream(S_DN1 + 22 * j, (low_banks, high_banks)[j % 2], WIDE, FT, hs_tile, None if j else hidden_wait,
                       place=22 * j % RING, after={9: [lambda: turn_block(j - 1)]} if j else None)
            pe.wait_ge(row_ready, 3)
            for half in range(2):
                pe.wait_ge(last_added, half + 1)
                turn_rows(3, (2 * half, 2 * half + 1)).then_inc(row_made, 1)

        @block.scalar
        def _(act):
            def split(first, slots, per_loop=0, i=0, at=0):
                for j in range(at, at + slots):
                    n = first + per_loop * i + j
                    act.wait_ge(loaded[j % RING], 16 * ((first + j) // RING + 1) + 16 * (per_loop // RING) * i)
                    if first + j >= RING:
                        act.wait_ge(slot_used, n - (RING - 1))
                    nc.scalar.activation(w_hi[:, j % RING, :], stage[:, j % RING, :], ACT.Copy).then_inc(hi_done, 1)

            def take_cross(banks, dst, n_done, sem_out, count=P):
                act.wait_ge(slot_used, n_done)
                b0, b1 = banks
                nc.scalar.activation(dst, ps[0:count, b0:b1, TOK:], ACT.Copy).then_inc(sem_out, 1)

            def stat(no):
                act.wait_ge(stat_made, no + 1)
                act.wait_ge(const_set, 2)
                nc.scalar.activation(rms[:, :], ps[:, 7, 0:TOK], ACT.Sqrt, bias=eps[:, 0:1]).then_inc(stat_root, 1)

            def res_square(rb):
                act.wait_ge(res_added, rb + 1)
                if not isinstance(rb, int) or rb:
                    act.wait_ge(sums_done, rb)
                j4 = 4 * (rb % 4)
                nc.scalar.activation(square[:, :, :], res[:, j4:j4 + 4, :], ACT.Square).then_inc(res_squared, 1)

            def res_high(rb):
                act.wait_ge(res_gained, rb + 1)
                j4 = 4 * (rb % 4)
                nc.scalar.activation(xs[:, j4:j4 + 4, 0:TOK], gated[:, :, :], ACT.Copy).then_inc(res_hi, 1)

            def steps_between(first, slots, steps, per_loop=0, i=0, at=0):
                for j in range(slots):
                    split(first, 1, per_loop, i, at + j)
                    for step in steps.get(j, ()):
                        step()

            act.dma_start(gain.ap(), gains).then_inc(in_gain, 16)

            def x_copy(j):
                act.wait_ge(x_turned, j + 1)
                b = X_BANKS[j % 2]
                nc.scalar.activation(res[:, 4 * j:4 * j + 4, :].rearrange("p m t -> p (m t)"),
                                     ps[:, b:b + 2, :].rearrange("p b c -> p (b c)"), ACT.Copy).then_inc(res_added, 1)

            x_copy(0)
            for j in range(4):
                if j < 3:
                    x_copy(j + 1)
                act.wait_ge(res_gained, j + 1)
                nc.scalar.activation(xs[:, 4 * j:4 * j + 4, 0:TOK], X_GAINED[j % 2][:, :, :],
                                     ACT.Copy).then_inc(res_hi, 1)
                for n in (2 * j, 2 * j + 1):
                    act.wait_ge(loaded[n % RING], 16 * (n // RING + 1))
                    if n >= RING:
                        act.wait_ge(slot_used, n - (RING - 1))
                    w = START_WIDTHS[n % 2]
                    nc.scalar.activation(w_hi[:, n % RING, 0:w], stage[:, n % RING, 0:w], ACT.Copy).then_inc(hi_done, 1)
                res_square(j)
                if j == 0:
                    for dst, src in ((tab, tables), (mat_a, mats[:, 2:7, :]), (bound, bounds), (hgain, head_gains),
                                     (taps, conv_taps)):
                        act.dma_start(dst.ap(), src).then_inc(in_small, 16)

            def ki_halves():
                act.wait_ge(slot_used, 7)
                nc.scalar.activation(cross[0:80, 0, :], ps[0:80, 4, TOK:], ACT.Copy).then_inc(ki_cross, 1)

            def weights_of_heads():
                act.wait_ge(ki_turned, 1)
                nc.scalar.activation(wt[:, :, :], ps[:, 5, 0:TOK].rearrange("p (a c) -> p a c", a=2)[:, :, ID:ID + IH],
                                     ACT.Copy, scale=IH ** -0.5 * ID ** -0.5).then_inc(wt_ready, 1)

            def qi_halves(i):
                act.wait_ge(qi_summed, i + 1)
                take_cross(QI_BANKS[i % 2], cross[:, 0:2, :], S_QI + 4 * i + 4, qi_cross)

            def relu(i):
                act.wait_ge(score_made, i + 1)
                act.wait_ge(score_step, 8 * i + 1)
                nc.scalar.activation(index_scores[:, :, :], ps[:, 4:8, 0:384], ACT.Relu).then_inc(rel_done, 1)

            def qkv_halves(g, u):
                if u == 0 and isinstance(g, int):
                    act.wait_ge(qi_summed, 5)
                else:
                    act.wait_ge(qkv_summed, 3 * g + u)
                take_cross(STREAM_BANKS[u], cross[:, 0:2, :], S_QKV + 12 * g + 4 * u + 4, qkv_cross)

            def gain_k(g):
                act.wait_ge(qkv_scaled, 3 * g + 1)
                if isinstance(g, int):
                    act.wait_ge(ki_ready, 1)
                    act.wait_ge(in_small, 80)
                else:
                    act.wait_ge(k_roped, g)
                nc.scalar.activation(k_sq[:, :], raw[:, 0, :], ACT.Square).then_inc(k_squared, 1)
                nc.scalar.activation(k_gn[:, :], raw[:, 0, :], ACT.Copy, scale=hgain[:, 1:2]).then_inc(k_gained, 1)

            def gain_q(g, u):
                act.wait_ge(qkv_scaled, 3 * g + 2 + u)
                if u == 0 and isinstance(g, int):
                    act.wait_ge(qi_ready, 4)
                elif not isinstance(g, int) or g:
                    act.wait_ge(q_cos, g)
                    act.wait_ge(q_var, g)
                nc.scalar.activation(square[:, 2 * u:2 * u + 2, :], raw[:, 2 + 2 * u:4 + 2 * u, :],
                                     ACT.Square).then_inc(q_squared, 1)
                nc.scalar.activation(gated[:, 2 * u:2 * u + 2, :], raw[:, 2 + 2 * u:4 + 2 * u, :], ACT.Copy,
                                     scale=hgain[:, 0:1]).then_inc(q_gained, 1)

            def root_k(p):
                act.wait_ge(k_made, p + 1)
                nc.scalar.activation(k_rt[:, :], ps[:, 4, 0:TOK], ACT.Sqrt, bias=eps[:, 0:1]).then_inc(k_root, 1)

            def values(p):
                act.wait_ge(v_made, p + 1)
                nc.scalar.activation(vt[:, :, :], ps[:, 5, 0:TOK].rearrange("p (a c) -> p a c", a=2),
                                     ACT.Copy).then_inc(v_ready, 1)

            def root_q(p):
                act.wait_ge(q_var, p + 1)
                nc.scalar.activation(q_rt[:, :, :], ps[:, 5, 0:8].rearrange("p (a h) -> p a h", a=2), ACT.Sqrt,
                                     bias=eps[:, 1:2], scale=float(HD)).then_inc(q_root, 1)

            def exps(p):
                for a in range(2):
                    act.wait_ge(npeak_done, 2 * p + a + 1)
                    for h in range(REP):
                        nc.scalar.activation(prob[:, chunk(a, h)], prob[:, chunk(a, h)], ACT.Exp,
                                             bias=npeak[:, a, h:h + 1],
                                             accum_out=den[:, a, h:h + 1]).then_inc(exp_done, 1)

            def copy_pt(p):
                for a, (c0, c1) in enumerate(((0, 512), (512, 1536))):
                    act.wait_ge(pt_made, 2 * p + a + 1)
                    nc.scalar.activation(pt[:, c0:c1], ps_heads[:, c0:c1], ACT.Copy).then_inc(pt_copied, 1)

            def out_high(p):
                for a in range(2):
                    act.wait_ge(o_made, 2 * p + a + 1)
                    nc.scalar.activation(hs[:, bass.ds(4 * p, 4), a * P:(a + 1) * P],
                                         ps[:, 4 + a, :].rearrange("p (h q) -> p h q", h=4), ACT.Copy).then_inc(o_hi, 1)

            def kv_q01_steps(g):
                return {7: [lambda: qkv_halves(g, 0)],
                        11: [lambda: qkv_halves(g, 1), lambda: gain_k(g), lambda: gain_q(g, 0)]}

            def head_steps(p, at):
                steps = ([lambda: qkv_halves(p, 2)], [lambda: root_k(p), lambda: gain_q(p, 1), lambda: values(p)],
                         [lambda: root_q(p)], [lambda: exps(p)], [lambda: copy_pt(p)])
                return merged(*({slot: some} for slot, some in zip(at, steps)))

            def group(g, steps):
                for j in range(12):
                    if j < RING:
                        act.wait_ge(v_loaded[j], 16 * g + 16)
                    split(S_QKV, 1, 12, g, j)
                    for step in steps.get(j, ()):
                        step()

            index_steps = {6: [ki_halves, lambda: stat(0)], 7: [lambda: qi_halves(0)], 9: [weights_of_heads],
                           11: [lambda: qi_halves(1)], 12: [lambda: relu(0)], 15: [lambda: qi_halves(2)]}
            steps_between(S_QI, INDEX_SLOTS - 4, {at - 4: some for at, some in index_steps.items()}, at=4)
            group(0, merged({0: [lambda: relu(1)], 3: [lambda: qi_halves(3)], 4: [lambda: relu(2)]},
                            kv_q01_steps(0), {7: [lambda: relu(3)]}))
            with act.Fori(1, KV) as g:
                group(g, merged(head_steps(g - 1, (1, 3, 5, 8, 11)), kv_q01_steps(g), {11: [lambda: out_high(g - 1)]}))
            last_head_steps = merged(head_steps(KV - 1, (1, 1, 2, 5, 7)), {7: [lambda: out_high(KV - 1)]})

            low_banks, high_banks = (0, 4), (4, 8)

            def res_steps(rb, n_done, last=False):
                def halves():
                    act.wait_ge(res_added, rb)
                    take_cross((low_banks, high_banks)[rb % 2], cross[:, :, :], n_done, res_cross)
                if last:
                    return {3: [halves]}
                if rb % 4 == 3:
                    return {3: [halves], 4: [lambda: res_high(rb), lambda: res_square(rb)]}
                return {3: [halves], 4: [lambda: res_square(rb)], 5: [lambda: res_high(rb)]}

            def project(first, q, tiles, before):
                slots = tiles // 2
                for j in range(4):
                    steps_between(first, slots, before, at=slots * j)
                    before = res_steps(4 * q + j, first + slots * (j + 1), last=q == 4)
                return before

            def hidden_tiles(fb):
                return hs[:, bass.ds(4 * fb, 4), 0:TOK]

            def gate_steps(fb, done, n_done):
                def halves():
                    if done or not isinstance(fb, int) or fb:
                        act.wait_ge(up_summed, fb + done)
                    take_cross(low_banks, cross[:, :, :], n_done, gate_cross)

                def silu():
                    act.wait_ge(gate_scaled, fb + done + 1)
                    nc.scalar.activation(gated[:, :, :], gated[:, :, :], ACT.Silu).then_inc(gate_silu, 1)
                return {11: [halves], 12: [silu]}

            def up_steps(fb, done, n_done):
                def halves():
                    act.wait_ge(gate_summed, fb + done + 1)
                    take_cross(high_banks, cross[:, :, :], n_done, up_cross)

                def high():
                    act.wait_ge(hidden_done, fb + done + 1)
                    nc.scalar.activation(hidden_tiles(fb), total[:, :, :], ACT.Copy).then_inc(hidden_hi, 1)
                return {3: [halves], 4: [high]}

            def ffn(layer, first, q, before):
                done = FT // 4 * layer
                steps_between(first, 16, before | {10: [lambda: stat(q)]} | gate_steps(0, done, first + 8))
                with act.Fori(1, FT // 4) as i:
                    steps = up_steps(i - 1, done, first + 16 * i) | gate_steps(i, done, first + 16 * i + 8)
                    steps_between(first, 16, steps, 16, i)
                return up_steps(FT // 4 - 1, done, first + 16 * (FT // 4))

            def conv_steps(i, u, n_done):
                def halves():
                    if isinstance(i, int) and i == 0 and u == 0:
                        act.wait_ge(res_added, 12)
                    else:
                        act.wait_ge(cv_summed, 3 * i + u)
                    take_cross((2 * u, 2 * u + 2), cross[:, 0:2, :], n_done, cv_cross)

                def high():
                    act.wait_ge(y_done, i + 1)
                    nc.scalar.activation(hs[:, bass.ds(2 * i, 2), 0:TOK], total[:, 0:2, :], ACT.Copy).then_inc(y_hi, 1)
                return {(7, 11, 3)[u]: [halves]} | ({4: [high]} if u == 2 else {})

            def conv(before):
                steps_between(S_CV, 12, before | conv_steps(0, 0, S_CV + 4) | {10: [lambda: stat(2)]}
                              | conv_steps(0, 1, S_CV + 8))
                with act.Fori(1, 8) as i:
                    n = S_CV + 12 * i
                    steps_between(S_CV, 12, conv_steps(i - 1, 2, n) | conv_steps(i, 0, n + 4)
                                  | conv_steps(i, 1, n + 8), 12, i)
                return conv_steps(7, 2, S_CO)

            before = project(S_AO, 1, KT, last_head_steps)
            before = ffn(0, S_GU0, 1, before)
            before = project(S_DN0, 2, FT, before)
            before = conv(before)
            before = project(S_CO, 3, KT, before)
            before = ffn(1, S_GU1, 3, before)
            def row_copy(j):
                act.wait_ge(row_made, j + 1)
                b = 4 * (j % 2)
                nc.scalar.activation(rows[j], ps[:, b:b + 2, :], ACT.Copy).then_inc(row_ready, 1)

            for j in range(4):
                steps_between(S_DN1, 22, merged(before, {12: [lambda: row_copy(j - 1)]} if j else {}), at=22 * j)
                before = res_steps(16 + j, S_DN1 + 22 * (j + 1), last=True)
            act.wait_ge(slot_used, S_END)
            act.wait_ge(res_added, 19)
            for half in range(2):
                nc.scalar.activation(cross[:, 2 * half:2 * half + 2, :], ps[:, 4 + 2 * half:6 + 2 * half, TOK:],
                                     ACT.Copy).then_inc(last_cross, 1)
            act.wait_ge(row_made, 5)
            nc.scalar.activation(rows[3][:, 0, :], ps[:, 0, :], ACT.Copy).then_inc(row_ready, 1)

        @block.vector
        def _(dve):
            tt = nc.vector.tensor_tensor

            def split(first, slots, per_loop=0, i=0, at=0):
                for j in range(at, at + slots):
                    n = first + per_loop * i + j
                    dve.wait_ge(hi_done, n + 1)
                    p = j % RING
                    tt(w_lo[:, p, :], stage[:, p, :], f32(w_hi[:, p, :]), ALU.subtract).then_inc(lo_done, 1)

            def steps_between(first, slots, steps, per_loop=0, i=0, at=0):
                for j in range(slots):
                    split(first, 1, per_loop, i, at + j)
                    for step in steps.get(j, ()):
                        step()

            def stat_sum_step(no):
                dve.wait_ge(sums_done, 4 * no + 4)
                nc.vector.tensor_reduce(colsum[:, :], sums[:, :, :].rearrange("p m t -> p t m"), AX_X,
                                        ALU.add).then_inc(stat_sum, 1)

            def rstd_step(no):
                dve.wait_ge(stat_root, no + 1)
                nc.vector.reciprocal(rstd[:, :], rms[:, :]).then_inc(rstd_ready, 1)

            def res_gain(rb):
                dve.wait_ge(res_added, rb + 1)
                q, j = divmod(rb, 4)
                tt(gated[:, :, :], res[:, 4 * j:4 * j + 4, :], per_tile(gain[:, q, 4 * j:4 * j + 4], TOK),
                   ALU.mult).then_inc(res_gained, 1)

            def res_low(rb):
                dve.wait_ge(res_hi, rb + 1)
                j4 = 4 * (rb % 4)
                tt(xs[:, j4:j4 + 4, TOK:], gated[:, :, :], f32(xs[:, j4:j4 + 4, 0:TOK]),
                   ALU.subtract).then_inc(xs_ready, 1)

            def res_sums(rb):
                dve.wait_ge(res_squared, rb + 1)
                if rb % 4:
                    dve.wait_ge(sums_done, rb)
                    tt(sums[:, :, :], sums[:, :, :], square[:, :, :], ALU.add).then_inc(sums_done, 1)
                else:
                    nc.vector.tensor_copy(sums[:, :, :], square[:, :, :]).then_inc(sums_done, 1)

            def res_steps(rb):
                q, j = divmod(rb, 4)
                bank = 4 * (rb % 2)

                def add():
                    dve.wait_ge(res_cross, rb - 3)
                    tt(total[:, :, :], ps[:, bank:bank + 4, 0:TOK], cross[:, :, :], ALU.add).then_inc(res_summed, 1)
                    dve.wait_ge(res_summed, rb - 3)
                    now = res[:, 4 * j:4 * j + 4, :]
                    tt(now, now, total[:, :, :], ALU.add).then_inc(res_added, 1)
                if q == 4:
                    return {3: [add]}
                steps = {3: [add], 4: [lambda: res_gain(rb)], 5: [lambda: res_low(rb)],
                         6: [lambda: res_sums(rb)]}
                if j == 3:
                    return {3: [add, lambda: res_gain(rb)], 4: [lambda: res_low(rb)],
                            5: [lambda: res_sums(rb), lambda: stat_sum_step(q)]}
                return steps

            def project(first, q, tiles, before):
                slots = tiles // 2
                for j in range(4):
                    steps_between(first, slots, before, at=slots * j)
                    before = res_steps(4 * q + j)
                return before

            def x_gain(j):
                dve.wait_ge(res_added, j + 1)
                if j >= 2:
                    dve.wait_ge(xs_ready, j - 1)
                tt(X_GAINED[j % 2][:, :, :], res[:, 4 * j:4 * j + 4, :], per_tile(gain[:, 0, 4 * j:4 * j + 4], TOK),
                   ALU.mult).then_inc(res_gained, 1)

            dve.wait_ge(in_gain, 16)
            x_gain(0)
            for j in range(4):
                if j < 3:
                    x_gain(j + 1)
                dve.wait_ge(res_hi, j + 1)
                tt(xs[:, 4 * j:4 * j + 4, TOK:], X_GAINED[j % 2][:, :, :], f32(xs[:, 4 * j:4 * j + 4, 0:TOK]),
                   ALU.subtract).then_inc(xs_ready, 1)
                for n in (2 * j, 2 * j + 1):
                    dve.wait_ge(hi_done, n + 1)
                    p, w = n % RING, START_WIDTHS[n % 2]
                    tt(w_lo[:, p, 0:w], stage[:, p, 0:w], f32(w_hi[:, p, 0:w]), ALU.subtract).then_inc(lo_done, 1)
            dve.wait_ge(in_small, 80)

            def ki_sum():
                dve.wait_ge(ki_cross, 1)
                tt(kiwi[0:80, :], ps[0:80, 4, 0:TOK], cross[0:80, 0, :], ALU.add).then_inc(qi_summed, 1)

            def ki_scale():
                dve.wait_ge(qi_summed, 1)
                dve.wait_ge(rstd_ready, 1)
                tt(kiwi[0:80, :], kiwi[0:80, :], rstd[0:80, :], ALU.mult).then_inc(ki_scaled, 1)

            def ki_rope():
                dve.wait_ge(ki_turned, 1)
                tt(kir[:, :], ps[:, 6, 0:TOK], COS_I, ALU.mult).then_inc(ki_cos, 1)
                tt(k_sq[:, :], ps[:, 6, TOK:], SIN_I, ALU.mult).then_inc(ki_sin, 1)
                dve.wait_ge(ki_cos, 1)
                dve.wait_ge(ki_sin, 1)
                tt(kir[:, :], kir[:, :], k_sq[:, :], ALU.add).then_inc(ki_ready, 1)
                nc.vector.memset(score[:, :], 0.0).then_inc(score_step, 1)

            def qi_sum(i):
                two = total[:, 0:2, :]
                b0, b1 = QI_BANKS[i % 2]
                dve.wait_ge(qi_cross, i + 1)
                if i:
                    dve.wait_ge(qi_turned, i)
                tt(two, ps[:, b0:b1, 0:TOK], cross[:, 0:2, :], ALU.add).then_inc(qi_summed, 1)
                dve.wait_ge(qi_summed, i + 2)
                tt(two, two, bcast(rstd[:, :], 2), ALU.mult).then_inc(qi_scaled, 1)
                dve.wait_ge(qi_scaled, i + 1)
                tt(gated[:, 0:2, :], two, bcast(COS_I, 2), ALU.mult).then_inc(qi_cos, 1)

            def qi_rope(i):
                dve.wait_ge(qi_turned, i + 1)
                tt(square[:, 0:2, :], ps[:, 7, :].rearrange("p (m t) -> p m t", m=2), bcast(SIN_I, 2),
                   ALU.mult).then_inc(qi_sin, 1)
                dve.wait_ge(qi_cos, i + 1)
                dve.wait_ge(qi_sin, i + 1)
                if i:
                    dve.wait_ge(score_made, i)
                tt(qir[:, :, :], gated[:, 0:2, :], square[:, 0:2, :], ALU.add).then_inc(qi_ready, 1)

            def add_scores(i):
                dve.wait_ge(wt_ready, 1)
                dve.wait_ge(rel_done, i + 1)
                for h in range(4):
                    for a, (c0, c1) in enumerate(COLS):
                        dve.wait_ge(score_step, 8 * i + max(1, 2 * h + a))
                        nc.vector.scalar_tensor_tensor(score[:, c0:c1], index_scores[:, h, c0:c1],
                                                       wt[:, a, 4 * i + h:4 * i + h + 1], score[:, c0:c1],
                                                       ALU.mult, ALU.add).then_inc(score_step, 1)

            def top(count):
                dve.wait_ge(top_step, count)

            def bound_scores():
                dve.wait_ge(score_step, 33)
                tt(score[:, :], score[:, :], bound[:, 0, :], ALU.min).then_inc(top_step, 1)

            def top_rounds(rounds):
                for r in rounds:
                    for a, (c0, c1) in enumerate(COLS):
                        top(max(1, 4 * r + a))
                        nc.vector.max(top8[:, r, a, :], score[:, c0:c1]).then_inc(top_step, 1)
                    for a, (c0, c1) in enumerate(COLS):
                        top(4 * r + 2 + a)
                        nc.vector.match_replace(score[:, c0:c1], top8[:, r, a, :], score[:, c0:c1],
                                                TAKEN).then_inc(top_step, 1)

            def make_mask():
                top(TOPK // 2 + 1)
                nc.vector.tensor_scalar(mask[:, :], score[:, :], TAKEN, -DROP, ALU.is_equal,
                                        ALU.mult).then_inc(top_step, 1)
                top(TOPK // 2 + 2)
                nc.vector.tensor_scalar(mask[:, :], mask[:, :], DROP, None, ALU.add).then_inc(top_step, 1)
                top(TOPK // 2 + 3)
                tt(mask[:, :], mask[:, :], bound[:, 1, :], ALU.min).then_inc(mask_ready, 1)

            def qkv_sum(g, u):
                b0, b1 = STREAM_BANKS[u]
                two = raw[:, 2 * u:2 * u + 2, :]
                dve.wait_ge(qkv_cross, 3 * g + u + 1)
                if not isinstance(g, int) or g:
                    if u == 0:
                        dve.wait_ge(v_made, g)
                        dve.wait_ge(k_gained, g)
                    else:
                        dve.wait_ge(q_gained, 2 * g + u - 2)
                tt(two, ps[:, b0:b1, 0:TOK], cross[:, 0:2, :], ALU.add).then_inc(qkv_summed, 1)
                dve.wait_ge(qkv_summed, 3 * g + u + 1)
                tt(two, two, bcast(rstd[:, :], 2), ALU.mult).then_inc(qkv_scaled, 1)

            def rope_k(p):
                dve.wait_ge(k_root, p + 1)
                tt(k_sq[:, :], ps[:, 4, TOK:], SIN_H, ALU.mult).then_inc(k_sin, 1)
                nc.vector.reciprocal(k_rt[:, :], k_rt[:, :]).then_inc(k_inv, 1)
                dve.wait_ge(k_cos, p + 1)
                dve.wait_ge(k_sin, p + 1)
                tt(kr[:, :], kr[:, :], k_sq[:, :], ALU.add).then_inc(k_roped, 1)
                dve.wait_ge(k_roped, p + 1)
                dve.wait_ge(k_inv, p + 1)
                tt(kr[:, :], kr[:, :], k_rt[:, :], ALU.mult).then_inc(k_ready, 1)

            def sin_q(p, u):
                dve.wait_ge(q_turned, 2 * p + u + 1)
                tt(sums[:, 2 * u:2 * u + 2, :], ps[:, 6 + u, :].rearrange("p (m t) -> p m t", m=2),
                   bcast(SIN_H, 2), ALU.mult).then_inc(q_sin, 1)

            def rope_q(p):
                dve.wait_ge(q_cos, p + 1)
                dve.wait_ge(q_sin, 2 * p + 2)
                tt(qr[:, :, :], qr[:, :, :], sums[:, :, :], ALU.add).then_inc(q_ready, 1)

            def logit(p):
                dve.wait_ge(q_root, p + 1)
                nc.vector.reciprocal(q_rt[:, :, :], q_rt[:, :, :]).then_inc(q_inv, 1)
                dve.wait_ge(q_inv, p + 1)
                dve.wait_ge(mask_ready, 1)
                for a, (c0, c1) in enumerate(COLS):
                    dve.wait_ge(s_made, 2 * p + a + 1)
                    for h in range(REP):
                        nc.vector.scalar_tensor_tensor(prob[:, chunk(a, h)], ps_heads[:, chunk(a, h)],
                                                       q_rt[:, a, h:h + 1], mask[:, c0:c1],
                                                       ALU.mult, ALU.add).then_inc(logit_ready, 1)
                    dve.wait_ge(logit_ready, 8 * p + 4 * a + 4)
                    nc.vector.tensor_reduce(peak[:, a, :], heads(prob, a), AX_X, ALU.max).then_inc(peak_done, 1)
                    dve.wait_ge(peak_done, 2 * p + a + 1)
                    nc.vector.tensor_scalar(npeak[:, a, :], peak[:, a, :], -1.0, None, ALU.mult).then_inc(npeak_done, 1)

            def normalise(p):
                for a, (c0, c1) in enumerate(COLS):
                    dve.wait_ge(exp_done, 8 * p + 4 * a + 4)
                    nc.vector.reciprocal(rden[:, a, :], den[:, a, :]).then_inc(rden_done, 1)
                    dve.wait_ge(rden_done, 2 * p + a + 1)
                    tt(heads(prob, a), heads(prob, a), per_tile(rden[:, a, :], c1 - c0), ALU.mult).then_inc(prob_ready, 1)

            def out_low(p):
                tiles = bass.ds(4 * p, 4)
                for a in range(2):
                    dve.wait_ge(o_hi, 2 * p + a + 1)
                    tt(hs[:, tiles, TOK + a * P:TOK + (a + 1) * P], ps[:, 4 + a, :].rearrange("p (h q) -> p h q", h=4),
                       f32(hs[:, tiles, a * P:(a + 1) * P]), ALU.subtract).then_inc(o_read, 1)

            def kv_q01_steps(g):
                return {7: [lambda: qkv_sum(g, 0)], 11: [lambda: qkv_sum(g, 1)]}

            def head_steps(p, at):
                steps = ([lambda: qkv_sum(p, 2)], [lambda: rope_k(p), lambda: sin_q(p, 0)],
                         [lambda: sin_q(p, 1), lambda: rope_q(p)], [lambda: logit(p)], [lambda: normalise(p)],
                         [lambda: out_low(p)])
                return merged(*({slot: some} for slot, some in zip(at, steps)))

            index_steps = {5: [lambda: stat_sum_step(0)], 6: [ki_sum, lambda: rstd_step(0), ki_scale],
                           7: [lambda: qi_sum(0)], 9: [ki_rope],
                           10: [lambda: qi_rope(0)], 11: [lambda: qi_sum(1)], 12: [lambda: add_scores(0)],
                           14: [lambda: qi_rope(1)], 15: [lambda: qi_sum(2)]}
            steps_between(S_QI, INDEX_SLOTS - 4, {at - 4: some for at, some in index_steps.items()}, at=4)
            steps_between(S_QKV, 12, merged(
                kv_q01_steps(0),
                {0: [lambda: add_scores(1)], 2: [lambda: qi_rope(2)], 3: [lambda: qi_sum(3)],
                 4: [lambda: add_scores(2)], 6: [lambda: qi_rope(3)],
                 7: [lambda: add_scores(3), bound_scores], 8: [lambda: top_rounds((0,))],
                 9: [lambda: top_rounds((1,))], 10: [lambda: top_rounds((2,))],
                 11: [lambda: top_rounds((3,))]}))
            steps_between(S_QKV + 12, 12, merged(
                kv_q01_steps(1), head_steps(0, (1, 3, 5, 6, 8, 11)),
                {2: [lambda: top_rounds((4, 5))], 4: [lambda: top_rounds((6,))],
                 5: [lambda: top_rounds((7,)), make_mask]}))
            with dve.Fori(2, KV) as g:
                steps_between(S_QKV, 12, merged(kv_q01_steps(g), head_steps(g - 1, (1, 3, 5, 6, 8, 11))), 12, g)
            last_head_steps = head_steps(KV - 1, (1, 1, 1, 5, 5, 7))

            def gate_sum(fb, done):
                dve.wait_ge(gate_cross, fb + done + 1)
                tt(gated[:, :, :], ps[:, 0:4, 0:TOK], cross[:, :, :], ALU.add).then_inc(gate_summed, 1)

            def gate_scale(fb, done):
                dve.wait_ge(gate_summed, fb + done + 1)
                tt(gated[:, :, :], gated[:, :, :], bcast(rstd[:, :], 4), ALU.mult).then_inc(gate_scaled, 1)

            def up_sum(fb, done):
                dve.wait_ge(up_cross, fb + done + 1)
                tt(total[:, :, :], ps[:, 4:8, 0:TOK], cross[:, :, :], ALU.add).then_inc(up_summed, 1)
                dve.wait_ge(up_summed, fb + done + 1)
                tt(total[:, :, :], total[:, :, :], bcast(rstd[:, :], 4), ALU.mult).then_inc(up_scaled, 1)
                dve.wait_ge(up_scaled, fb + done + 1)
                dve.wait_ge(gate_silu, fb + done + 1)
                tt(total[:, :, :], total[:, :, :], gated[:, :, :], ALU.mult).then_inc(hidden_done, 1)

            def hidden_low(fb, done):
                dve.wait_ge(hidden_hi, fb + done + 1)
                tiles = bass.ds(4 * fb, 4)
                tt(hs[:, tiles, TOK:], total[:, :, :], f32(hs[:, tiles, 0:TOK]), ALU.subtract).then_inc(hidden_ready, 1)

            def gate_steps(fb, done):
                return {11: [lambda: gate_sum(fb, done), lambda: gate_scale(fb, done)]}

            def up_steps(fb, done):
                return {3: [lambda: up_sum(fb, done)], 5: [lambda: hidden_low(fb, done)]}

            def ffn(layer, first, q, before):
                done = FT // 4 * layer
                steps_between(first, 16, before | {10: [lambda: rstd_step(q)]} | gate_steps(0, done))
                with dve.Fori(1, FT // 4) as i:
                    steps_between(first, 16, up_steps(i - 1, done) | gate_steps(i, done), 16, i)
                return up_steps(FT // 4 - 1, done)

            def conv_sum(i, u):
                dst = gated if u == 0 else total
                dve.wait_ge(cv_cross, 3 * i + u + 1)
                tt(dst[:, 0:2, :], ps[:, 2 * u:2 * u + 2, 0:TOK], cross[:, 0:2, :], ALU.add).then_inc(cv_summed, 1)

            def conv_scale(i, u):
                dst = gated if u == 0 else total
                dve.wait_ge(cv_summed, 3 * i + u + 1)
                tt(dst[:, 0:2, :], dst[:, 0:2, :], bcast(rstd[:, :], 2), ALU.mult).then_inc(cv_scaled, 1)

            def conv_z(i):
                dve.wait_ge(cv_scaled, 3 * i + 2)
                if isinstance(i, int):
                    dve.wait_ge(zeros_set, 1)
                tt(z[:, :, 2:TOK + 2], gated[:, 0:2, :], total[:, 0:2, :], ALU.mult).then_inc(z_ready, 1)

            def conv_taps(i, which):
                dve.wait_ge(z_ready, i + 1)
                for t in which:
                    for m in range(2):
                        tap = taps[:, t, bass.ds(2 * i + m, 1)]
                        src = z[:, m, t:t + TOK]
                        if t == 0:
                            ins = nc.vector.tensor_scalar(ytap[:, m, :], src, tap, None, ALU.mult)
                        else:
                            dve.wait_ge(tap_step, 6 * i + 2 * t + m - 1)
                            ins = nc.vector.scalar_tensor_tensor(ytap[:, m, :], src, tap, ytap[:, m, :],
                                                                 ALU.mult, ALU.add)
                        ins.then_inc(tap_step, 1)

            def conv_gate(i):
                dve.wait_ge(cv_scaled, 3 * i + 3)
                dve.wait_ge(tap_step, 6 * i + 6)
                tt(total[:, 0:2, :], total[:, 0:2, :], ytap[:, :, :], ALU.mult).then_inc(y_done, 1)

            def conv_low(i):
                dve.wait_ge(y_hi, i + 1)
                tiles = bass.ds(2 * i, 2)
                tt(hs[:, tiles, TOK:], total[:, 0:2, :], f32(hs[:, tiles, 0:TOK]), ALU.subtract).then_inc(y_ready, 1)

            def c_steps(i):
                return {7: [lambda: conv_sum(i, 0), lambda: conv_scale(i, 0)]}

            def u_steps(i):
                return {11: [lambda: conv_sum(i, 1), lambda: conv_scale(i, 1), lambda: conv_z(i)]}

            def b_steps(i):
                return {0: [lambda: conv_taps(i, (0, 1))], 1: [lambda: conv_taps(i, (2,))],
                        3: [lambda: conv_sum(i, 2), lambda: conv_scale(i, 2), lambda: conv_gate(i)],
                        5: [lambda: conv_low(i)]}

            def conv(before):
                steps_between(S_CV, 12, before | {7: [lambda: conv_sum(0, 0)],
                                                  10: [lambda: rstd_step(2), lambda: conv_after_stat()]} | u_steps(0))
                with dve.Fori(1, 8) as i:
                    steps_between(S_CV, 12, b_steps(i - 1) | c_steps(i) | u_steps(i), 12, i)
                return b_steps(7)

            def conv_after_stat():
                dve.wait_ge(rstd_ready, 3)
                conv_scale(0, 0)
                nc.vector.memset(z[:, :, 0:2], 0.0).then_inc(zeros_set, 1)

            before = project(S_AO, 1, KT, last_head_steps)
            before = ffn(0, S_GU0, 1, before)
            before = project(S_DN0, 2, FT, before)
            before = conv(before)
            before = project(S_CO, 3, KT, before)
            before = ffn(1, S_GU1, 3, before)
            project(S_DN1, 4, FT, before)
            for half in range(2):
                tiles = slice(2 * half, 2 * half + 2)
                dve.wait_ge(last_cross, half + 1)
                tt(total[:, tiles, :], ps[:, 4 + 2 * half:6 + 2 * half, 0:TOK], cross[:, tiles, :],
                   ALU.add).then_inc(last_summed, 1)
                dve.wait_ge(last_summed, half + 1)
                now = res[:, 12 + 2 * half:14 + 2 * half, :]
                tt(now, now, total[:, tiles, :], ALU.add).then_inc(last_added, 1)
            dve.wait_ge(row_made, 5)
            nc.vector.tensor_copy(rows[3][:, 1, :], ps[:, 1, :]).then_inc(row_ready_dve, 1)

        @block.gpsimd
        def _(pool):
            pool.memset(eps[:, 0:1], EPS).then_inc(const_set, 1)
            pool.memset(eps[:, 1:2], EPS * HD).then_inc(const_set, 1)
            for j in range(4):
                pool.wait_ge(res_squared, j + 1)
                if j:
                    pool.wait_ge(sums_done, j)
                    nc.gpsimd.tensor_tensor(sums[:, :, :], sums[:, :, :], square[:, :, :], ALU.add).then_inc(sums_done, 1)
                else:
                    nc.gpsimd.tensor_copy(sums[:, :, :], square[:, :, :]).then_inc(sums_done, 1)
            pool.wait_ge(in_small, 80)

            def cos_products(g):
                pool.wait_ge(k_gained, g + 1)
                if not isinstance(g, int):
                    pool.wait_ge(s_made, 2 * g)
                nc.gpsimd.tensor_tensor(kr[:, :], k_gn[:, :], COS_H, ALU.mult).then_inc(k_cos, 1)
                pool.wait_ge(q_gained, 2 * g + 2)
                nc.gpsimd.tensor_tensor(qr[:, :, :], gated[:, :, :], bcast(COS_H, 4), ALU.mult).then_inc(q_cos, 1)
            cos_products(0)
            with pool.Fori(1, KV) as g:
                cos_products(g)


def shape_constants():
    tables = np.zeros((P, 4, TOK), np.float32)
    pos = np.arange(TOK, dtype=np.float32)
    for at, dim in ((0, HD), (2, ID)):
        inv = np.float32(1.0) / np.float32(10000.0) ** (np.arange(0, dim, 2, dtype=np.float32) / np.float32(dim))
        angle = (pos[None, :] * inv[:, None]).astype(np.float32).astype(np.float64)
        rows = np.arange(P) % (dim // 2)
        tables[:, at] = np.cos(angle)[rows]
        tables[:, at + 1] = np.sin(angle)[rows]

    def rotation(dim):
        r = np.zeros((P, P), np.float32)
        for m in range(P):
            first = m % dim < dim // 2
            r[m + dim // 2 if first else m - dim // 2, m] = -1.0 if first else 1.0
        return r

    dup = np.zeros((P, P), np.float32)
    for m in range(P):
        dup[m % ID, m] = 1.0
    dup_rot = np.zeros((P, P), np.float32)
    rot = rotation(ID)
    for m in range(P):
        dup_rot[:ID, m] = rot[:ID, m % ID]
    mats = np.stack([np.eye(P, dtype=np.float32), np.full((P, P), 1.0 / D, np.float32),
                     np.full((P, P), 1.0 / HD, np.float32), rotation(HD), rotation(ID), dup, dup_rot], axis=1)
    bounds = np.zeros((P, 2, 384), np.float32)
    for a, (c0, c1) in enumerate(COLS):
        query = a * P + np.arange(P)[:, None]
        key = np.arange(c1 - c0)[None, :]
        bounds[:, 0, c0:c1] = np.where(key <= query, np.float32(-FILL), np.float32(FILL))
        bounds[:, 1, c0:c1] = np.where(key <= query, np.float32(0.0), np.float32(DROP))
    return tables, np.ascontiguousarray(mats), bounds


def kernel(x, attn_norm, attn_w_in, attn_q_norm, attn_k_norm, attn_w_out, conv_norm, conv_w_in, conv_w,
           conv_w_out, ffn_norm, ffn_w_gate, ffn_w_up, ffn_w_down):
    import concourse.bacc as bacc
    from concourse.bass_utils import run_bass_kernel_spmd

    def by_partition(a):
        a = np.asarray(a).reshape(-1, KT, P)
        return np.ascontiguousarray(a.transpose(2, 0, 1))

    x, attn_norm, conv_norm, ffn_norm = (np.asarray(a) for a in (x, attn_norm, conv_norm, ffn_norm))
    tables, mats, bounds = shape_constants()
    arrays = {
        "x": x[0],
        "attn_w_in": attn_w_in[0], "attn_w_out": attn_w_out[0],
        "conv_w_in": conv_w_in[0], "conv_w_out": conv_w_out[0],
        "w_gate": ffn_w_gate, "w_up": ffn_w_up, "w_down": ffn_w_down,
        "gains": by_partition(np.stack([attn_norm[0], ffn_norm[0], conv_norm[0], ffn_norm[1]])),
        "head_gains": np.stack([np.asarray(attn_q_norm)[0], np.asarray(attn_k_norm)[0]], axis=1),
        "conv_taps": by_partition(np.asarray(conv_w)[0]),
        "tables": tables, "mats": mats, "bounds": bounds,
    }
    arrays = {f"in_{k}": np.ascontiguousarray(v) for k, v in arrays.items()}
    nc = bacc.Bacc("TRN2", target_bir_lowering=False, num_devices=1)
    args = [nc.dram_tensor(k, v.shape, mybir.dt.from_np(v.dtype), kind="ExternalInput").ap() for k, v in arrays.items()]
    out = nc.dram_tensor("out", (TOK, D), F32, kind="ExternalOutput").ap()
    trunk(nc, *args, out)
    r = run_bass_kernel_spmd(nc, [arrays], core_ids=[0])
    return np.asarray(r.results[0]["out"]).reshape(1, TOK, D)
```
